# Optimizing a Trainium2 kernel written in Bass

```python
import math
import jax, jax.numpy as jnp
from jax import lax
import numpy as np

D_MODEL = 2048
BATCH = 1
SEQ = 512
DEPTH = 1
DEC_BATCH = 8
DEC_SEQ = 1
PAST_LEN = 512
PAGE_SIZE = 128

ATTN_WIDTH = D_MODEL // 2
POOL_WIDTH = D_MODEL - ATTN_WIDTH
N_HEADS = 8
HEAD_DIM = ATTN_WIDTH // N_HEADS // 2
N_QK_HEADS = 2 * N_HEADS
V_DIM = 2 * HEAD_DIM
POOL_WINDOWS = (2, 4, 8, 16)
N_POOL_GROUPS = len(POOL_WINDOWS)
POOL_GROUP = POOL_WIDTH // N_POOL_GROUPS
POOL_STATE = max(POOL_WINDOWS) - 1
PROJ_WIDTH = 3 * ATTN_WIDTH + POOL_WIDTH
D_FF = -(-(8 * D_MODEL) // (3 * 256)) * 256
PLE_DIM = 256
ROPE_THETA = 10000.0
Q_BLOCK = 128
EPS = 1e-6

kernel_name = "hybrid_diffattn_multiscale_pool_decoder_step"

def rmsnorm(x, g):
    xf = x.astype(jnp.float32)
    y = xf * lax.rsqrt(jnp.mean(xf * xf, axis=-1, keepdims=True) + EPS)
    return (y * g.astype(jnp.float32)).astype(x.dtype)

def rope(x, pos):
    half = HEAD_DIM // 2
    inv = ROPE_THETA ** (-jnp.arange(half, dtype=jnp.float32) / half)
    ang = pos.astype(jnp.float32)[:, None] * inv[None, :]
    cos = jnp.cos(ang)[:, None, :]
    sin = jnp.sin(ang)[:, None, :]
    xf = x.astype(jnp.float32)
    x1, x2 = xf[..., :half], xf[..., half:]
    return jnp.concatenate([x1 * cos - x2 * sin, x2 * cos + x1 * sin], axis=-1).astype(x.dtype)

def diff_lambda(lq1, lk1, lq2, lk2, lam_init):
    f = jnp.float32
    return (jnp.exp(jnp.sum(lq1.astype(f) * lk1.astype(f)))
            - jnp.exp(jnp.sum(lq2.astype(f) * lk2.astype(f))) + lam_init)

def prompt_diff_attention(q, k, v, lam):
    B, S = q.shape[0], q.shape[1]
    nb = S // Q_BLOCK
    scale = HEAD_DIM ** -0.5
    qb = q.reshape(B, nb, Q_BLOCK, N_HEADS, 2, HEAD_DIM).swapaxes(0, 1)
    kpos = jnp.arange(S)

    def one_block(args):
        qi, bi = args
        s = jnp.einsum('bqhcd,bkhcd->bhcqk', qi, k, preferred_element_type=jnp.float32) * scale
        qpos = bi * Q_BLOCK + jnp.arange(Q_BLOCK)
        mask = kpos[None, :] <= qpos[:, None]
        a = jax.nn.softmax(jnp.where(mask, s, -jnp.inf), axis=-1)
        w = a[:, :, 0] - lam * a[:, :, 1]
        o = jnp.einsum('bhqk,bkhe->bqhe', w.astype(v.dtype), v, preferred_element_type=jnp.float32)
        return o.astype(v.dtype)

    o = lax.map(one_block, (qb, jnp.arange(nb)))
    return o.swapaxes(0, 1).reshape(B, S, N_HEADS, V_DIM)

def sample_diff_attention(q, k_new, v_new, k_past, v_past, lam):
    DS = q.shape[1]
    P = k_past.shape[1]
    scale = HEAD_DIM ** -0.5
    s_past = jnp.einsum('bqhcd,bkhcd->bhcqk', q, k_past, preferred_element_type=jnp.float32) * scale
    s_new = jnp.einsum('bqhcd,bkhcd->bhcqk', q, k_new, preferred_element_type=jnp.float32) * scale
    causal = jnp.arange(DS)[None, :] <= jnp.arange(DS)[:, None]
    s = jnp.concatenate([s_past, jnp.where(causal, s_new, -jnp.inf)], axis=-1)
    a = jax.nn.softmax(s, axis=-1)
    w = (a[:, :, 0] - lam * a[:, :, 1]).astype(v_new.dtype)
    o = (jnp.einsum('bhqk,bkhe->bqhe', w[..., :P], v_past, preferred_element_type=jnp.float32)
         + jnp.einsum('bhqk,bkhe->bqhe', w[..., P:], v_new, preferred_element_type=jnp.float32))
    return o.astype(v_new.dtype)

def pool_mixer(u, prefix, pos0, w_pool, pool_scale):
    B, S, C = u.shape
    ext = jnp.concatenate([prefix, u], axis=1)
    cs = jnp.cumsum(ext.astype(jnp.float32), axis=1)
    cs = jnp.concatenate([jnp.zeros((B, 1, C), jnp.float32), cs], axis=1)
    L = POOL_STATE + 1
    pos = pos0 + jnp.arange(S)
    outs = []
    for g, win in enumerate(POOL_WINDOWS):
        sl = slice(g * POOL_GROUP, (g + 1) * POOL_GROUP)
        wsum = cs[:, L:L + S, sl] - cs[:, L - win:L - win + S, sl]
        cnt = jnp.minimum(pos + 1, win).astype(jnp.float32)[None, :, None]
        pooled = wsum / cnt - u[..., sl].astype(jnp.float32)
        outs.append(jnp.einsum('bsc,cd->bsd', pooled.astype(u.dtype), w_pool[g]))
    out = jnp.concatenate(outs, axis=-1) * pool_scale
    return out, ext[:, -POOL_STATE:]

def run_layer(h, p_i, pos0, pool_prefix, attend, lam_init,
              g_mix, w_in, w_out, lq1, lk1, lq2, lk2, g_sub, w_pool, pool_scale,
              g_ffn, w_gate_up, w_down, g_ple, w_ple_gate, w_ple_proj):
    B, S, _ = h.shape
    xn = rmsnorm(h, g_mix)
    proj = xn @ w_in
    q, k, v, u = jnp.split(proj, [ATTN_WIDTH, 2 * ATTN_WIDTH, 3 * ATTN_WIDTH], axis=-1)
    pos = pos0 + jnp.arange(S)
    q = rope(q.reshape(B, S, N_QK_HEADS, HEAD_DIM), pos)
    k = rope(k.reshape(B, S, N_QK_HEADS, HEAD_DIM), pos)
    v = v.reshape(B, S, N_HEADS, V_DIM)
    lam = diff_lambda(lq1, lk1, lq2, lk2, lam_init)
    o = attend(q.reshape(B, S, N_HEADS, 2, HEAD_DIM), k.reshape(B, S, N_HEADS, 2, HEAD_DIM), v, lam)
    o = (rmsnorm(o, g_sub) * (1.0 - lam_init)).reshape(B, S, ATTN_WIDTH)
    pool_out, pool_state = pool_mixer(u, pool_prefix, pos0, w_pool, pool_scale)
    h = h + jnp.concatenate([o, pool_out], axis=-1) @ w_out
    gate, up = jnp.split(rmsnorm(h, g_ffn) @ w_gate_up, 2, axis=-1)
    h = h + (jax.nn.silu(gate) * up) @ w_down
    h = h + jax.nn.sigmoid(rmsnorm(h, g_ple) @ w_ple_gate) * (p_i @ w_ple_proj)
    return h, k, v, pool_state

def setup_inputs(seed: int = 0) -> dict:
    key = jax.random.key(seed)
    ks = jax.random.split(key, 32)
    f = jnp.float32
    n_pages = PAST_LEN // PAGE_SIZE
    n_used = DEC_BATCH * n_pages
    n_pool = n_used + n_used // 4
    nrm = lambda i, shape, s: jax.random.normal(ks[i], shape, f) * s
    page_table = jax.random.permutation(ks[7], n_pool)[:n_used].reshape(DEC_BATCH, n_pages).astype(jnp.int32)
    return {
        "x_prompt": nrm(0, (BATCH, SEQ, D_MODEL), 1.0),
        "x_sample": nrm(1, (DEC_BATCH, DEC_SEQ, D_MODEL), 1.0),
        "p_prompt": nrm(2, (DEPTH, BATCH, SEQ, PLE_DIM), 1.0),
        "p_sample": nrm(3, (DEPTH, DEC_BATCH, DEC_SEQ, PLE_DIM), 1.0),
        "cache_k": nrm(4, (DEPTH, n_pool, PAGE_SIZE, N_QK_HEADS, HEAD_DIM), 1.0),
        "cache_v": nrm(5, (DEPTH, n_pool, PAGE_SIZE, N_HEADS, V_DIM), 1.0),
        "state_pool": nrm(6, (DEPTH, DEC_BATCH, POOL_STATE, POOL_WIDTH), 1.0),
        "page_table": page_table,
        "g_mix": 1.0 + nrm(8, (DEPTH, D_MODEL), 0.02),
        "w_in": nrm(9, (DEPTH, D_MODEL, PROJ_WIDTH), D_MODEL ** -0.5),
        "w_out": nrm(10, (DEPTH, D_MODEL, D_MODEL), D_MODEL ** -0.5),
        "lambda_q1": nrm(11, (DEPTH, HEAD_DIM), 0.1),
        "lambda_k1": nrm(12, (DEPTH, HEAD_DIM), 0.1),
        "lambda_q2": nrm(13, (DEPTH, HEAD_DIM), 0.1),
        "lambda_k2": nrm(14, (DEPTH, HEAD_DIM), 0.1),
        "g_sub": 1.0 + nrm(15, (DEPTH, V_DIM), 0.02),
        "w_pool": nrm(16, (DEPTH, N_POOL_GROUPS, POOL_GROUP, POOL_GROUP), POOL_GROUP ** -0.5),
        "pool_scale": 1.0 + nrm(17, (DEPTH, POOL_WIDTH), 0.02),
        "g_ffn": 1.0 + nrm(18, (DEPTH, D_MODEL), 0.02),
        "w_gate_up": nrm(19, (DEPTH, D_MODEL, 2 * D_FF), D_MODEL ** -0.5),
        "w_down": nrm(20, (DEPTH, D_FF, D_MODEL), D_FF ** -0.5),
        "g_ple": 1.0 + nrm(21, (DEPTH, D_MODEL), 0.02),
        "w_ple_gate": nrm(22, (DEPTH, D_MODEL, D_MODEL), D_MODEL ** -0.5),
        "w_ple_proj": nrm(23, (DEPTH, PLE_DIM, D_MODEL), PLE_DIM ** -0.5),
        "g_final": 1.0 + nrm(24, (D_MODEL,), 0.02),
    }

def reference(x_prompt, x_sample, p_prompt, p_sample, cache_k, cache_v, state_pool, page_table,
              g_mix, w_in, w_out, lambda_q1, lambda_k1, lambda_q2, lambda_k2, g_sub, w_pool, pool_scale,
              g_ffn, w_gate_up, w_down, g_ple, w_ple_gate, w_ple_proj, g_final):
    n_dec = x_sample.shape[0]
    past_len = page_table.shape[1] * cache_k.shape[2]
    hp, hs = x_prompt, x_sample
    kp_l, vp_l, pp_l, ks_l, vs_l, ps_l = [], [], [], [], [], []
    for li in range(DEPTH):
        lam_init = 0.8 - 0.6 * math.exp(-0.3 * li)
        params = (g_mix[li], w_in[li], w_out[li], lambda_q1[li], lambda_k1[li], lambda_q2[li],
                  lambda_k2[li], g_sub[li], w_pool[li], pool_scale[li], g_ffn[li], w_gate_up[li],
                  w_down[li], g_ple[li], w_ple_gate[li], w_ple_proj[li])
        prefix0 = jnp.zeros((hp.shape[0], POOL_STATE, POOL_WIDTH), hp.dtype)
        hp, k_p, v_p, pool_p = run_layer(hp, p_prompt[li], 0, prefix0, prompt_diff_attention,
                                         lam_init, *params)
        k_past = cache_k[li][page_table].reshape(n_dec, past_len, N_HEADS, 2, HEAD_DIM)
        v_past = cache_v[li][page_table].reshape(n_dec, past_len, N_HEADS, V_DIM)
        attend_s = lambda q, k, v, lam, kp=k_past, vp=v_past: sample_diff_attention(q, k, v, kp, vp, lam)
        hs, k_s, v_s, pool_s = run_layer(hs, p_sample[li], past_len, state_pool[li], attend_s,
                                         lam_init, *params)
        kp_l.append(k_p); vp_l.append(v_p); pp_l.append(pool_p)
        ks_l.append(k_s); vs_l.append(v_s); ps_l.append(pool_s)
    y_prompt = rmsnorm(hp, g_final)
    y_sample = rmsnorm(hs, g_final)
    return (y_prompt, y_sample, jnp.stack(kp_l), jnp.stack(vp_l), jnp.stack(pp_l),
            jnp.stack(ks_l), jnp.stack(vs_l), jnp.stack(ps_l))


_drawn_inputs = setup_inputs


def setup_inputs(seed=0):
    import zlib

    import numpy as np

    out = dict(_drawn_inputs(seed))
    spreads = {}
    factors = {'g_mix': 2.839,
     'lambda_k2': 3.322,
     'g_sub': 6.166,
     'pool_scale': 5.886,
     'g_ffn': 4.995,
     'g_ple': 8.0,
     'g_final': 2.827}
    for name, (base, spread) in spreads.items():
        noise = np.random.default_rng([zlib.crc32(name.encode()), seed]).standard_normal(out[name].shape)
        drawn = base * np.exp(spread * noise) if base else spread * noise
        out[name] = __import__('jax').numpy.asarray(drawn.astype(out[name].dtype))
    for name, factor in factors.items():
        out[name] = (out[name] * factor).astype(out[name].dtype)
    return out
```

```python
from contextlib import ExitStack

import numpy as np

import concourse.bass as bass
from concourse import mybir

ALU = mybir.AluOpType
ACT = mybir.ActivationFunctionType
AX = mybir.AxisListType
F32 = mybir.dt.float32
F32R = mybir.dt.float32r
I32 = mybir.dt.int32
ds = bass.ds

P = 128
D = 2048
SEQ = 512
NB = 8
T = SEQ + NB
HT = T // 2
KD = D // P
NH = 8
HD = 64
AW = NH * P
PW = D - AW
PT = PW // P
WINDOWS = (2, 4, 8, 16)
PS = max(WINDOWS) - 1
DFF = 5632
PLE = 256
PAST = 512
PAGE = 128
NPG = PAST // PAGE
EPS = 1e-6
LAM0 = 0.8 - 0.6
SCALE = HD ** -0.5
NEG = -1e30
SL = 16 * P
CH = 4
NCH = DFF // P // CH

QKV_N, VU_N = 0, 2 * NH
POOL_N = VU_N + 2 * NH
OUT_N = POOL_N + 1
FFN_N = OUT_N + KD
FFN_STEP = 3 * CH
PLE_N = FFN_N + NCH * FFN_STEP
SLABS = PLE_N + KD
POOL_T = VU_N + 2 * NH
OUT_T = POOL_T + PT
FFN_T = OUT_T + KD
FFN_TSTEP = 2 * CH + KD
PLE_T = FFN_T + NCH * FFN_TSTEP

C_ID, C_MASK, C_ONE, C_INV = 0, 128, 256, 384
C_WIN = C_INV + PT * 16
C_SEL = C_WIN + PT * 4
C_PAIR = C_SEL + len(WINDOWS) * NB
C_SGN = C_PAIR + NH
C_EPS = C_SGN + 2
C_ALL = C_EPS + 1

V_MIX, V_FFN, V_PLE, V_FINAL, V_POOL, V_SUB = 0, 16, 32, 48, 64, 72
V_ALL = 73

EV = 13
MAIL_VU = NH + 1
E_QB, E_TR01, E_SAM, E_TR23, E_W, E_PV, E_OT, E_PT, E_VN = 0, 2, 4, 5, 7, 8, 10, 11, 12


def mail(g, e):
    return MAIL_VU + EV * g + e


def constants():
    c = np.zeros((P, C_ALL), np.float32)
    c[:, C_ID:C_ID + P] = np.eye(P, dtype=np.float32)
    c[:, C_MASK:C_MASK + P] = np.where(np.arange(P)[None, :] <= np.arange(P)[:, None], 0.0, NEG)
    c[:, C_ONE:C_ONE + P] = 1.0
    for t in range(PT):
        win = WINDOWS[t * len(WINDOWS) // PT]
        c[:, C_INV + 16 * t:C_INV + 16 * (t + 1)] = 1.0 / np.minimum(np.arange(16) + 1, win)
        c[:, C_WIN + 4 * t:C_WIN + 4 * t + 4] = [win >= 4, win >= 8, win >= 16, 1.0 / win]
    for g, win in enumerate(WINDOWS):
        for b in range(NB):
            c[b * PS + PS - (win - 1):(b + 1) * PS, C_SEL + g * NB + b] = 1.0
    for r in range(2 * NH):
        c[r, C_PAIR + r // 2] = 1.0
        c[r, C_SGN + r % 2] = 1.0
    c[:, C_EPS] = EPS
    return c


def rope_tables():
    half = HD // 2
    inv = np.float32(10000.0) ** (-np.arange(half, dtype=np.float32) / np.float32(half))
    pos = np.concatenate([np.arange(SEQ), np.full(NB, PAST)]).astype(np.float32)
    ang = (inv[:, None] * pos[None, :]).astype(np.float32)
    cos, sin = np.cos(ang), np.sin(ang)
    return np.stack([np.concatenate([cos] * 4), np.concatenate([-sin, sin] * 2)], 1).astype(np.float32)


class Slab:

    def __init__(self, number, half=0):
        self.index = number + 2 * half
        self.slot = number % 2
        self.turn = number // 2 + half


class Steps:

    def __init__(self, eng, sem):
        self.eng, self.sem, self.base, self.k, self.last = eng, sem, 0, 0, None

    def step(self, ins):
        self.k += 1
        ins.then_inc(self.sem, 1)
        self.last = (self.sem, self.base + self.k)

    def says(self, ins, sem, value):
        ins.then_inc(sem, 1)
        self.last = (sem, value)

    def wait(self):
        self.eng.wait_ge(*self.last)

    def loop(self, start, end, per):
        outer = self.base + self.k
        with self.eng.Fori(start, end) as i:
            self.base, self.k = outer + (i - start) * per, 0
            yield i
            assert self.k == per, (self.k, per)
        self.base, self.k = outer + (end - start) * per, 0


def is_first(i):
    return isinstance(i, int) and i == 0


def halves(ap):
    return ap.rearrange("p (a b) -> p a b", a=2)


def layer(nc, x_prompt, x_sample, p_prompt, p_sample, cache_k, cache_v, state_pool, page_table,
          g_mix, w_in, w_out, lq1, lk1, lq2, lk2, g_sub, w_pool, pool_scale, g_ffn, w_gate_up,
          w_down, g_ple, w_ple_gate, w_ple_proj, g_final, const, rope,
          y_prompt, y_sample, k_prompt, v_prompt, pool_prompt, k_sample, v_sample, pool_sample):
    h_spill = nc.dram_tensor("h_spill", (P, KD * T), F32, kind="Internal").ap()
    w_in_v = w_in[0].rearrange("(k p) n -> p k n", p=P)
    w_out_v = w_out[0].rearrange("(k p) n -> p k n", p=P)
    w_gu_v = w_gate_up[0].rearrange("(k p) n -> p k n", p=P)
    w_dn_v = w_down[0].rearrange("(k p) n -> p k n", p=P)
    w_pg_v = w_ple_gate[0].rearrange("(k p) n -> p k n", p=P)
    w_pp_v = w_ple_proj[0].rearrange("(k p) n -> p k n", p=P)
    w_pool_v = w_pool[0].rearrange("g (k p) n -> p (g k) n", p=P)
    k_pages = cache_k[0].rearrange("n t h d -> n t (h d)")
    v_pages = cache_v[0].rearrange("n t h d -> n t (h d)")

    with ExitStack() as ctx:
        def sb(name, shape, dt=F32, where=ctx):
            return where.enter_context(nc.sbuf_tensor(name, shape, dt))

        def ps(name, shape):
            return ctx.enter_context(nc.psum_tensor(name, shape, F32))

        def sem(name):
            return ctx.enter_context(nc.semaphore(name))

        raw = [sb(f"raw{i}", [P, SL]) for i in range(2)]
        wh = [sb(f"w_high{i}", [P, SL], F32R) for i in range(2)]
        wl = [sb(f"w_low{i}", [P, SL], F32R) for i in range(2)]
        xh = sb("x_high", [P, KD, T], F32R)
        xl = sb("x_low", [P, KD, T], F32R)
        rstd = sb("rstd", [P, T])
        sums = sb("sums", [P, 4 * T])
        C = sb("constants", [P, C_ALL])
        gains = sb("gains", [P, V_ALL])
        neglam = sb("neglam", [P, 1])
        region = sb("region", [P, 2 * KD * T])
        with ExitStack() as early:
            k_now = sb("k_now", [P, T], where=early)
            q_now = sb("q_now", [P, T], where=early)
            v_now = sb("v_now", [P, T], where=early)
            v_nat = sb("v_nat", [P, SEQ], where=early)
            nat = sb("nat", [P, T], where=early)
            small = sb("small", [P, 1560], where=early)
        act_h = sb("act_high", [P, CH, T], F32R)
        act_l = sb("act_low", [P, CH, T], F32R)

        ident = C[:, C_ID:C_ID + P]
        ones = C[:, C_ONE:C_ONE + P]
        eps = C[:, C_EPS:C_EPS + 1]

        acc_sq = [sums[:, i * T:(i + 1) * T] for i in range(2)]
        sq = [sums[:, (2 + i) * T:(3 + i) * T] for i in range(2)]
        cos_r, sin_r = sums[:, 0:T], sums[:, T:2 * T]
        u_row = [sums[:, i * (T + 16):(i + 1) * (T + 16)] for i in range(3)]

        q_all = region[:, 0:NH * T].rearrange("p (h t) -> p h t", h=NH)
        k_all = region[:, NH * T:2 * NH * T].rearrange("p (h t) -> p h t", h=NH)
        h_all = region[:, KD * T:2 * KD * T].rearrange("p (k t) -> p k t", k=KD)
        x_nat = [region[:, i * 2048:(i + 1) * 2048].rearrange("p (b n) -> p b n", b=4) for i in range(3)]
        xs_nat = region[0:NB, 3 * 2048:3 * 2048 + D]
        late = region[:, KD * T:]
        pages = late[:, 0:NPG * AW].rearrange("p (g n) -> p g n", g=NPG)
        qb = late[:, 4096:5120]
        probs = late[:, 5120:6144].rearrange("p (c k) -> p c k", c=2)
        w_row = late[:, 6144:6656]
        w_turn = [late[:, 6656:7168], small[:, 0:512]]
        s_row = late[0:16, 7168:7168 + PAST + 1]
        e_row = late[0:16, 7700:7700 + PAST + 1]
        state = region[0:NB * PS, 0:PW]
        nat_k, nat_v, nat_u = (late[:, 5120 + i * 1024:5120 + (i + 1) * 1024] for i in range(3))

        def part(start, n):
            return small[:, start:start + n]
        k_new = part(512, 64).rearrange("p (h b) -> p h b", h=NH)
        v_new = part(576, 64).rearrange("p (h b) -> p h b", h=NH)
        q_new = part(640, 64).rearrange("p (h b) -> p h b", h=NH)
        u_new = part(704, NH * 23).rearrange("p (h b) -> p h b", h=NH)
        prod_new = part(888, 128)
        s_new = small[0:16, 1016:1024]
        o_new = part(1024, 64).rearrange("p (b h) -> p b h", b=NB)
        w_new = part(1088, 64).rearrange("p (b h) -> p b h", b=NB)
        state_sum = part(1152, 64)
        q_col = part(1216, 8)
        s_past = part(1224, 64).rearrange("p (g n) -> p g n", g=NPG)
        w_past = part(1288, 40)
        diff16 = small[0:16, 1328:1336]
        diff16n = small[0:16, 1336:1344]
        sgnlam = small[0:16, 1344:1345]
        top16 = small[0:16, 1345:1346]
        sum16 = small[0:16, 1346:1347]
        inv16 = small[0:16, 1347:1348]
        top = part(1348, 2)
        esum = part(1350, 2)
        einv = part(1352, 2)
        o_ss = part(1354, 4)
        o_inv = part(1358, 4)
        o_root = part(1362, 4)
        gsub = part(1366, 1)
        v_squares = part(1368, 128)

        gate_row = [region[:, i * T:(i + 1) * T] for i in range(2)]
        silu_row = [region[:, (2 + i) * T:(3 + i) * T] for i in range(2)]
        up_row = region[:, 4 * T:5 * T]
        act_row = region[:, 5 * T:6 * T]
        hg_row = [region[:, (6 + i) * T:(7 + i) * T] for i in range(2)]
        ys_nat = region[0:NB, 8 * T:8 * T + D]
        p_nat = region[:, 8 * T + D:8 * T + D + 4 * PLE].rearrange("p (b n) -> p b n", b=4)
        ps_nat = silu_row[0][0:NB, 0:PLE]
        p_turn = region[:, 14 * T:16 * T].rearrange("p (k t) -> p k t", k=2)
        wp_raw = region[:, 8 * T + D:8 * T + D + 4 * P]
        fin = region[:, 8 * T + D + 4 * PLE:8 * T + D + 4 * PLE + 16]
        vec_nat = k_now[0:V_ALL, 0:P]
        lam_in = small[0:1, 0:4 * HD].rearrange("p (a d) -> p a d", a=4)
        lam_pr = small[0:1, 256:256 + 2 * HD].rearrange("p (a d) -> p a d", a=2)
        lam_s = small[0:1, 400:402]
        lam_e = small[0:1, 402:404]
        lam_d = small[0:1, 404:405]
        pt_sb = sb("page_table_sb", [1, NB * NPG], I32)

        acc = [ps(f"acc{i}", [P, 2, 512]) for i in range(2)]
        sc = ps("scores", [P, 2, 512])
        mbank = ps("mail_bank", [P, 512])
        obank = ps("o_bank", [P, 512])
        sc_t = sc[:, :, 0:HT]

        def out(t):
            return acc[t % 2][:, :, 0:HT]

        names = """
            w_low_done setup_landed gains_landed rope_landed x_turned state_landed misc_stored
            h_spilled x_low squared_dve dotted mail_ready naturals_stored onew_done h_loaded
            pooled_low p_landed wp_landed p_copied wp_low nat_stored v_stored y_stored acc_free
            acc_ready pool_summed dve_summed stats_ready setup_turned x_copied gains_ready
            state_summed state_ready lam_ready neglam_summed rotated mail_free staged root_ready
            exped scored qcol_ready combined o_scaled o_ready diff_ready v_ready new_products
            neglam_ready snew_ready naturals u_taken onew_squared onew_stats naturals_copied
            p_turned act_low_done proj_free proj_ready hg_ready y_taken y_turned p_low fin_stats
            act_step w_high_done x_high squared_pool lam_summed lam_exped swapped maxed multiplied
            s_ready s_maxed s_exped o_squared onew_root pooled_high pool_high silued act_product
            act_high_done wp_high p_high h_done squared fin_root fin_inv y_scaled dve_step k_stored
            new_taken pool_step""".split()
        S = {n: sem(n) for n in names}
        raw_landed = [sem(f"raw_landed{i}") for i in range(2)]
        x_landed = [sem(f"x_landed{i}") for i in range(4)]
        k_landed = [sem(f"k_page_landed{i}") for i in range(NPG)]
        v_landed = [sem(f"v_page_landed{i}") for i in range(NPG)]

        block = ctx.enter_context(nc.Block())

        def src_qk(j, s):
            return w_in_v[:, :, ds((NH * (1 - s) + j) * P, P)]

        def src_vu(h, s):
            return w_in_v[:, :, ds((NH * (2 + s) + h) * P, P)]

        @block.sync
        def _(sp):
            def load(slab, src, first=False):
                if not first:
                    sp.wait_ge(S["w_low_done"], slab.index - 1)
                k = src.shape[1]
                sp.dma_start(raw[slab.slot][:, :].rearrange("p (k n) -> p k n", k=k), src)\
                    .then_inc(raw_landed[slab.slot], 16)

            def load_pages(b, source, landed):
                for g in range(NPG):
                    page = sp.value_load(pt_sb[0:1, ds(b * NPG + g, 1)], min_val=0,
                                         max_val=cache_k.shape[1] - 1)
                    sp.dma_start(pages[:, g, :], source[ds(page, 1), :, :].rearrange("a t n -> t (a n)"))\
                        .then_inc(landed[g], 16)

            xp = x_prompt[0].rearrange("(b p) n -> p b n", p=P)
            sp.dma_start(C[:, :], const).then_inc(S["setup_landed"], 16)
            sp.dma_start(xs_nat, x_sample.rearrange("b s n -> (b s) n")).then_inc(S["setup_landed"], 16)
            sp.dma_start(x_nat[0], xp[:, :, 0:512]).then_inc(x_landed[0], 16)
            for v, at, n in ((g_mix[0], V_MIX, 16), (g_ffn[0], V_FFN, 16), (g_ple[0], V_PLE, 16),
                             (g_final, V_FINAL, 16), (pool_scale[0], V_POOL, 8), (g_sub[0], V_SUB, 1)):
                sp.dma_start(vec_nat[at:at + n, :], v.rearrange("(k p) -> k p", p=P))\
                    .then_inc(S["gains_landed"], 16)
            for i, v in enumerate((lq1, lk1, lq2, lk2)):
                sp.dma_start(lam_in[:, i, :], v).then_inc(S["gains_landed"], 16)
            sp.dma_start(pt_sb[:, :], page_table.rearrange("b n -> (b n)").rearrange("(a n) -> a n", a=1))\
                .then_inc(S["gains_landed"], 16)
            sp.dma_start(x_nat[1], xp[:, :, 512:1024]).then_inc(x_landed[1], 16)
            load(Slab(0), src_qk(0, 0), first=True)
            sp.dma_start(x_nat[2], xp[:, :, 1024:1536]).then_inc(x_landed[2], 16)
            load(Slab(1), src_qk(0, 1), first=True)
            sp.dma_start(q_now[:, :], rope[:, 0, :]).then_inc(S["rope_landed"], 16)
            sp.dma_start(nat[:, :], rope[:, 1, :]).then_inc(S["rope_landed"], 16)
            sp.wait_ge(S["x_turned"], 4)
            sp.dma_start(x_nat[0], xp[:, :, 1536:2048]).then_inc(x_landed[3], 16)
            sp.wait_ge(S["x_turned"], 8)
            sp.dma_start(region[0:NB * PS, 2048:2048 + PW], state_pool[0].rearrange("b s n -> (b s) n"))\
                .then_inc(S["state_landed"], 16)
            sp.dma_start(pool_sample[0, :, 0:PS - 1, :], state_pool[0, :, 1:PS, :])\
                .then_inc(S["misc_stored"], 16)
            sp.wait_ge(S["gains_landed"], 16 * 11)
            load(Slab(2), src_qk(1, 0))
            load(Slab(3), src_qk(1, 1))

            with sp.Fori(2, NH) as j:
                load(Slab(0, j), src_qk(j, 0))
                load(Slab(1, j), src_qk(j, 1))
            sp.wait_ge(S["h_spilled"], 16)
            sp.wait_ge(S["x_low"], KD)
            sp.wait_ge(S["squared_dve"], KD // 2)
            load_pages(0, k_pages, k_landed)
            load(Slab(VU_N), src_vu(0, 0))
            load(Slab(VU_N + 1), src_vu(0, 1))
            load(Slab(VU_N + 2), src_vu(1, 0))
            load(Slab(VU_N + 3), src_vu(1, 1))

            def vu_iteration(h, loads):
                g = h - 1
                load(*loads[0])
                load(*loads[1])
                sp.wait_ge(S["dotted"], NPG * (g + 1))
                load_pages(g, v_pages, v_landed)
                sp.wait_ge(S["mail_ready"], mail(g, E_PV + 1) + 1)
                load_pages(h, k_pages, k_landed)

            with sp.Fori(1, NH - 1) as h:
                vu_iteration(h, [(Slab(VU_N + 2 + s, h), src_vu(h + 1, s)) for s in (0, 1)])
            vu_iteration(NH - 1, [(Slab(POOL_N), w_pool_v), (Slab(OUT_N), w_out_v[:, :, 0:P])])
            sp.wait_ge(S["dotted"], NPG * NH)
            load_pages(NH - 1, v_pages, v_landed)

            def src_out(m):
                return w_out_v[:, :, ds(m * P, P)]
            sp.wait_ge(S["naturals_stored"], 16 * 4)
            sp.wait_ge(S["onew_done"], 1)
            for a in range(2):
                sp.dma_start(late[:, a * KD * T // 2:(a + 1) * KD * T // 2],
                             h_spill[:, a * KD * T // 2:(a + 1) * KD * T // 2]).then_inc(S["h_loaded"], 16)
            load(Slab(OUT_N + 1), src_out(1))
            sp.wait_ge(S["x_low"], KD + NH)
            sp.wait_ge(S["pooled_low"], PT)
            sp.dma_start(p_nat, p_prompt[0, 0].rearrange("(b p) n -> p b n", p=P)).then_inc(S["p_landed"], 16)
            sp.dma_start(ps_nat, p_sample[0].rearrange("b s n -> (b s) n")).then_inc(S["p_landed"], 16)
            with sp.Fori(1, KD // 2) as j:
                load(Slab(OUT_N, j), src_out(2 * j))
                load(Slab(OUT_N + 1, j), src_out(2 * j + 1))

            with sp.Fori(0, NCH) as c:
                with sp.Fori(0, CH) as j:
                    for s in (0, 1):
                        load(Slab(FFN_N + s, c * (FFN_STEP // 2) + j),
                             w_gu_v[:, :, ds(s * DFF + (c * CH + j) * P, P)])
                with sp.Fori(0, CH // 2) as i:
                    for s in (0, 1):
                        load(Slab(FFN_N + 2 * CH + s, c * (FFN_STEP // 2) + i),
                             w_dn_v[:, ds(c * CH, CH), ds((2 * i + s) * 4 * P, 4 * P)])

            def load_wp(j):
                sp.dma_start(wp_raw.rearrange("p (k n) -> p k n", k=2), w_pp_v[:, :, ds(j * 2 * P, 2 * P)])\
                    .then_inc(S["wp_landed"], 16)

            sp.wait_ge(S["p_copied"], 1)
            load_wp(0)
            with sp.Fori(0, KD // 2 - 1) as j:
                for s in (0, 1):
                    load(Slab(PLE_N + s, j), w_pg_v[:, :, ds((2 * j + s) * P, P)])
                sp.wait_ge(S["wp_low"], j + 1)
                load_wp(j + 1)
            for m in (KD - 2, KD - 1):
                load(Slab(PLE_N + m), w_pg_v[:, :, m * P:(m + 1) * P])
            sp.wait_ge(S["misc_stored"], 16)
            sp.wait_ge(S["naturals_stored"], 16 * 4)
            sp.wait_ge(S["nat_stored"], 16 * NH)
            sp.wait_ge(S["v_stored"], 16 * NH)
            sp.wait_ge(S["y_stored"], 16 * 5)

        @block.tensor
        def _(pe):
            def mm(o, l, r, start=True, stop=True):
                return pe.matmul(o, l, r, start=start, stop=stop)

            def product(pair, w_high, w_low, x_high, x_low, first, last):
                for n, (w, x) in enumerate(((w_high, x_high), (w_high, x_low), (w_low, x_high))):
                    for a in (0, 1):
                        ins = mm(pair[:, a, 0:HT], w, x[:, a * HT:(a + 1) * HT],
                                 start=first and n == 0, stop=last and n == 2)
                return ins

            def begin(slab, t, first=False):
                pe.wait_ge(S["w_low_done"], slab.index + 1)
                if not first:
                    pe.wait_ge(S["acc_free"], t - 1)

            def part_of(slab, pair, t, ks, waits=None):
                for k in ks:
                    if waits:
                        waits(k)
                    ins = product(pair, wh[slab.slot][:, k * P:(k + 1) * P],
                                  wl[slab.slot][:, k * P:(k + 1) * P],
                                  xh[:, k, :], xl[:, k, :], k == 0, k == KD - 1)
                    if k == KD - 1:
                        ins.then_inc(S["acc_ready"], 1)

            def whole(slab, pair, t, waits=None, first=False):
                begin(slab, t, first)
                part_of(slab, pair, t, range(KD), waits)

            def stats(phase):
                pe.wait_ge(S["pool_summed"], 7 * (phase + 1))
                pe.wait_ge(S["dve_summed"], 7 * (phase + 1))
                for a in (0, 1):
                    for i in (0, 1):
                        ins = mm(sc[:, a, 0:HT], ones, acc_sq[i][:, a * HT:(a + 1) * HT],
                                 start=i == 0, stop=i == 1)
                ins.then_inc(S["stats_ready"], 1)

            pe.wait_ge(S["setup_landed"], 32)
            for k in range(KD):
                ins = pe.transpose(mbank[:, k * NB:(k + 1) * NB], xs_nat[:, k * P:(k + 1) * P], ident[0:NB, 0:NB])
            ins.then_inc(S["setup_turned"], 1)
            pe.wait_ge(S["gains_landed"], 16 * 11)
            pe.transpose(obank[:, 0:V_ALL], vec_nat, ident[0:V_ALL, 0:V_ALL]).then_inc(S["setup_turned"], 1)

            for k in range(KD):
                if k % 4 == 0:
                    pe.wait_ge(x_landed[k // 4], 16)
                if k >= 2:
                    pe.wait_ge(S["x_copied"], k - 1)
                for b in range(4):
                    ins = pe.transpose(sc[:, k % 2, b * P:(b + 1) * P],
                                       x_nat[k // 4 % 3][:, b, k % 4 * P:(k % 4 + 1) * P], ident)
                ins.then_inc(S["x_turned"], 1)
            pe.wait_ge(S["state_landed"], 16)
            pe.wait_ge(S["gains_ready"], 1)
            for t in range(PT):
                g = t * len(WINDOWS) // PT
                ins = mm(obank[:, t * NB:(t + 1) * NB], region[0:NB * PS, 2048 + t * P:2048 + (t + 1) * P],
                         C[0:NB * PS, C_SEL + g * NB:C_SEL + (g + 1) * NB])
            ins.then_inc(S["state_summed"], 1)
            pe.wait_ge(S["state_ready"], 1)
            pe.wait_ge(S["lam_ready"], 1)
            mm(obank[:, 0:1], ones[0:1, :], lam_d).then_inc(S["neglam_summed"], 1)

            def x_waits(base):
                return lambda k: pe.wait_ge(S["x_low"], base + k + 1)

            def k_natural(j):
                pe.wait_ge(S["rotated"], 2 * j + 1)
                if is_first(j):
                    pe.wait_ge(S["gains_ready"], 1)
                else:
                    pe.wait_ge(S["mail_free"], j)
                for b in range(4):
                    ins = pe.transpose(mbank[:, b * P:(b + 1) * P], k_now[:, b * P:(b + 1) * P], ident)
                ins.then_inc(S["mail_ready"], 1)

            def qk_iteration(j, waits=None, first=False):
                k_slab, q_slab = Slab(0, j), Slab(1, j)
                whole(k_slab, acc[0], 2 * j, waits, first)
                if first:
                    stats(0)
                begin(q_slab, 2 * j + 1, first)
                part_of(q_slab, acc[1], 2 * j + 1, range(0, KD // 2))
                k_natural(j)
                part_of(q_slab, acc[1], 2 * j + 1, range(KD // 2, KD))

            qk_iteration(0, x_waits(0), first=True)
            with pe.Fori(1, NH) as j:
                qk_iteration(j)

            def scores(g, b):
                if b == 0:
                    pe.wait_ge(S["staged"], g + 1)
                pe.wait_ge(S["exped"], 4 * g + b + 1)
                n = (b + 1) * P
                for c in (0, 1):
                    r = slice(c * HD, (c + 1) * HD)
                    ins = mm(sc[:, c, 0:n], q_now[r, b * P:(b + 1) * P], k_now[r, 0:n])
                ins.then_inc(S["scored"], 1)

            def mail_turn(g, e):
                pe.wait_ge(S["mail_free"], mail(g, e))

            def spread_q(g, i):
                if i == 0:
                    pe.wait_ge(S["qcol_ready"], g + 1)
                mail_turn(g, E_QB + i)
                for n in range(4):
                    ins = mm(mbank[:, n * P:(n + 1) * P],
                             q_col[:, 4 * i + n:4 * i + n + 1].to_broadcast([P, P]), ident)
                ins.then_inc(S["mail_ready"], 1)

            def turn_w(g, b, e):
                pe.wait_ge(S["combined"], 4 * g + b + 2)
                mail_turn(g, e)
                for kb in range(b + 1):
                    ins = pe.transpose(mbank[:, kb * P:(kb + 1) * P], w_row[:, kb * P:(kb + 1) * P], ident)
                ins.then_inc(S["mail_ready"], 1)

            def values(g, b, e):
                pe.wait_ge(S["mail_free"], mail(g, e) + 1)
                if b == 0:
                    pe.wait_ge(S["o_scaled"], g + 1)
                for kb in range(b + 1):
                    ins = mm(obank[:, b * P:(b + 1) * P], w_turn[b % 2][:, kb * P:(kb + 1) * P],
                             v_nat[:, kb * P:(kb + 1) * P], start=kb == 0, stop=kb == b)
                ins.then_inc(S["o_ready"], 1)

            def turn_sample_scores(g):
                pe.wait_ge(S["dotted"], NPG * (g + 1))
                mail_turn(g, E_SAM)
                for n in range(NPG):
                    ins = pe.transpose(mbank[0:16, n * P:(n + 1) * P], s_past[:, n, :], ident)
                ins.then_inc(S["mail_ready"], 1)

            def sample_weights(g):
                pe.wait_ge(S["diff_ready"], g + 2)
                mail_turn(g, E_W)
                for n in range(NPG):
                    mm(mbank[:, n * NH:(n + 1) * NH], e_row[:, n * P:(n + 1) * P], diff16)
                mm(mbank[:, NPG * NH:(NPG + 1) * NH], ones[0:16, :], diff16n).then_inc(S["mail_ready"], 1)

            def sample_values(g, i):
                if i == 0:
                    for n in range(NPG):
                        pe.wait_ge(v_landed[n], 16 * (g + 1))
                mail_turn(g, E_PV + i)
                for n in range(NPG):
                    ins = mm(mbank[0:NH, :], w_past[:, n * NH:(n + 1) * NH], pages[:, n, i * 512:(i + 1) * 512],
                             start=n == 0, stop=n == NPG - 1)
                ins.then_inc(S["mail_ready"], 1)

            def turn_sample_values(g):
                mail_turn(g, E_PT)
                for h in range(NH):
                    ins = mm(mbank[:, h * NH:(h + 1) * NH],
                             w_turn[h // 4][0:NH, h % 4 * P:(h % 4 + 1) * P], ident[0:NH, 0:NH])
                ins.then_inc(S["mail_ready"], 1)

            def turn_o(g):
                pe.wait_ge(S["o_scaled"], g + 2)
                mail_turn(g, E_OT)
                for b in range(4):
                    ins = pe.transpose(mbank[:, b * P:(b + 1) * P], nat[:, b * P:(b + 1) * P], ident)
                ins.then_inc(S["mail_ready"], 1)

            def v_natural(h):
                pe.wait_ge(S["v_ready"], h + 1)
                pe.wait_ge(S["mail_free"], mail(h - 1, E_VN))
                for b in range(4):
                    ins = pe.transpose(mbank[:, b * P:(b + 1) * P], v_now[:, b * P:(b + 1) * P], ident)
                ins.then_inc(S["mail_ready"], 1)

            def attention(g, fill):
                scores(g, 0)
                spread_q(g, 0)
                fill(0)
                scores(g, 1)
                spread_q(g, 1)
                fill(1)
                turn_w(g, 0, E_TR01)
                fill(2)
                scores(g, 2)
                turn_w(g, 1, E_TR01 + 1)
                fill(3)
                values(g, 0, E_TR01)
                scores(g, 3)
                turn_sample_scores(g)
                fill(4)
                values(g, 1, E_TR01 + 1)
                turn_w(g, 2, E_TR23)
                fill(5)
                values(g, 2, E_TR23)
                turn_w(g, 3, E_TR23 + 1)
                sample_weights(g)
                fill(6)
                values(g, 3, E_TR23 + 1)
                sample_values(g, 0)
                fill(7)
                sample_values(g, 1)
                turn_o(g)
                turn_sample_values(g)

            def vu_iteration(h):
                v_slab, u_slab = Slab(VU_N, h), Slab(VU_N + 1, h)

                def fill(i):
                    slab, t, pair = (v_slab, VU_N + 2 * h, acc[0]) if i < 4 else (u_slab, VU_N + 1 + 2 * h, acc[1])
                    if i % 4 == 0:
                        begin(slab, t)
                    part_of(slab, pair, t, range(i % 4 * 4, i % 4 * 4 + 4))
                if is_first(h):
                    for i in range(8):
                        fill(i)
                else:
                    attention(h - 1, fill)
                v_natural(h)

            pe.wait_ge(S["new_products"], 1)
            pe.wait_ge(S["neglam_ready"], 1)
            for b in range(NB):
                ins = mm(obank[0:16, b:b + 1], prod_new[:, b * 16:(b + 1) * 16], ones[:, 0:1])
            ins.then_inc(S["snew_ready"], 1)

            vu_iteration(0)
            with pe.Fori(1, NH) as h:
                vu_iteration(h)
            attention(NH - 1, lambda i: None)

            pe.wait_ge(S["exped"], 4 * NH + 1)
            pe.wait_ge(S["mail_free"], mail(NH - 1, E_PT) + 1)
            for h in range(NH):
                ins = pe.transpose(sc[0:NB, h // 4, h % 4 * P:(h % 4 + 1) * P], k_new[:, h, :], ident)
            ins.then_inc(S["naturals"], 1)
            pe.wait_ge(S["acc_free"], VU_N + 2 * NH)
            for h in range(NH):
                ins = pe.transpose(acc[0][0:NB, h // 4, h % 4 * P:(h % 4 + 1) * P], v_new[:, h, :], ident)
            ins.then_inc(S["naturals"], 1)
            pe.wait_ge(S["u_taken"], 2 * NH)
            for h in range(NH):
                ins = pe.transpose(acc[1][0:23, h // 4, h % 4 * P:(h % 4 + 1) * P], u_new[:, h, :], ident)
            ins.then_inc(S["naturals"], 1)
            pe.wait_ge(S["onew_squared"], 1)
            mm(obank[:, 0:64], ones, v_squares[:, 0:64]).then_inc(S["onew_stats"], 1)

            pe.wait_ge(S["naturals_copied"], 3)
            pe.wait_ge(S["w_low_done"], POOL_N + 1)
            slab = Slab(POOL_N)
            for t in range(PT):
                g, m = divmod(t, 2)
                pe.wait_ge(S["pooled_low"], 2 * g + 2)
                pe.wait_ge(S["acc_free"], POOL_T + t - 1)
                for k in (0, 1):
                    at = (g * 2 + k) * 2 * P + m * P
                    ins = product(acc[t % 2], wh[slab.slot][:, at:at + P], wl[slab.slot][:, at:at + P],
                                  act_h[:, 2 * (g % 2) + k, :], act_l[:, 2 * (g % 2) + k, :], k == 0, k == 1)
                ins.then_inc(S["acc_ready"], 1)

            def out_waits(k):
                if k < NH:
                    pe.wait_ge(S["x_low"], KD + k + 1)
                else:
                    pe.wait_ge(S["acc_free"], POOL_T + k - NH + 1)
            whole(Slab(OUT_N), acc[0], OUT_T, out_waits)
            whole(Slab(OUT_N + 1), acc[1], OUT_T + 1)
            with pe.Fori(1, KD // 2) as j:
                whole(Slab(OUT_N, j), acc[0], OUT_T + 2 * j)
                whole(Slab(OUT_N + 1, j), acc[1], OUT_T + 1 + 2 * j)

            pe.wait_ge(S["p_landed"], 32)
            for k in (0, 1):
                bank = (mbank, obank)[k]
                for b in range(4):
                    pe.transpose(bank[:, b * P:(b + 1) * P], p_nat[:, b, k * P:(k + 1) * P], ident)
                ins = pe.transpose(sc[:, 0, k * NB:(k + 1) * NB], ps_nat[:, k * P:(k + 1) * P], ident[0:NB, 0:NB])
            ins.then_inc(S["p_turned"], 1)

            def gate_up(c, j, waits=None):
                for s in (0, 1):
                    whole(Slab(FFN_N + s, c * (FFN_STEP // 2) + j), acc[s],
                          FFN_T + s + c * FFN_TSTEP + 2 * j, waits if s == 0 else None)
                    if waits and s == 0:
                        pe.wait_ge(S["p_copied"], 1)
                        stats(1)

            def down(c, i):
                for s in (0, 1):
                    slab = Slab(FFN_N + 2 * CH + s, c * (FFN_STEP // 2) + i)
                    for m in range(4):
                        t = FFN_T + 2 * CH + 4 * s + m + c * FFN_TSTEP + 8 * i
                        if m == 0:
                            begin(slab, t)
                        else:
                            pe.wait_ge(S["acc_free"], t - 1)
                        for k in range(CH):
                            if s == 0 and m == 0:
                                pe.wait_ge(S["act_low_done"], c * CH + k + 1)
                            at = k * 4 * P + m * P
                            ins = product(acc[m % 2], wh[slab.slot][:, at:at + P], wl[slab.slot][:, at:at + P],
                                          act_h[:, k, :], act_l[:, k, :], k == 0, k == CH - 1)
                        ins.then_inc(S["acc_ready"], 1)

            gate_up(0, 0, x_waits(KD + NH))
            with pe.Fori(1, CH) as j:
                gate_up(0, j)
            with pe.Fori(0, CH // 2) as i:
                down(0, i)
            with pe.Fori(1, NCH) as c:
                with pe.Fori(0, CH) as j:
                    gate_up(c, j)
                with pe.Fori(0, CH // 2) as i:
                    down(c, i)

            def project(j, s):
                m = 2 * j + s
                if s == 0:
                    pe.wait_ge(S["wp_low"], j + 1)
                if s > 0 or not is_first(j):
                    pe.wait_ge(S["proj_free"], m)
                for k in (0, 1):
                    at = k * 2 * P + s * P
                    ins = product(sc, act_h[:, 2, at:at + P], act_l[:, 2, at:at + P],
                                  act_h[:, k, :], act_l[:, k, :], k == 0, k == 1)
                ins.then_inc(S["proj_ready"], 1)

            def turn_y(m, s):
                pe.wait_ge(S["hg_ready"], m + 1)
                if not is_first(m):
                    pe.wait_ge(S["y_taken"], m)
                for b in range(4):
                    pe.transpose(mbank[:, b * P:(b + 1) * P], hg_row[s][:, b * P:(b + 1) * P], ident)
                pe.transpose(obank[0:NB, 0:P], hg_row[s][:, SEQ:T], ident).then_inc(S["y_turned"], 1)

            def ple(j, first=False):
                for s in (0, 1):
                    slab, t = Slab(PLE_N + s, j), PLE_T + s + 2 * j
                    begin(slab, t)
                    part_of(slab, acc[s], t, range(0, KD // 2), x_waits(2 * KD + NH) if first and s == 0 else None)
                    if not (first and s == 0):
                        turn_y(2 * j + s - 1, 1 - s)
                    part_of(slab, acc[s], t, range(KD // 2, KD), x_waits(2 * KD + NH) if first and s == 0 else None)
                    if first and s == 0:
                        stats(2)
                        pe.wait_ge(S["p_low"], 2)
                        pe.wait_ge(S["root_ready"], 3)
                    project(j, s)

            ple(0, first=True)
            with pe.Fori(1, KD // 2) as j:
                ple(j)
            turn_y(KD - 1, 1)
            pe.wait_ge(S["pool_summed"], 7 * 3 + KD)
            pe.wait_ge(S["proj_free"], KD)
            for b in range(4):
                mm(sc[:, 0, b:b + 1], acc_sq[0][:, b * P:(b + 1) * P], ones[:, 0:1])
            mm(sc[0:NB, 0, 4:5], acc_sq[0][:, SEQ:T], ones[:, 0:1]).then_inc(S["fin_stats"], 1)

        @block.scalar
        def _(act):
            A = Steps(act, S["act_step"])

            def high(slab):
                act.wait_ge(raw_landed[slab.slot], 16 * (slab.turn + 1))
                act.activation(wh[slab.slot][:, :], raw[slab.slot][:, :], ACT.Copy).then_inc(S["w_high_done"], 1)

            def norm_split(phase, gain, h_ready):
                for k in range(KD):
                    h_ready(k)
                    act.activation(xh[:, k, :], h_all[:, k, :], ACT.Copy,
                                   scale=gains[:, gain + k:gain + k + 1]).then_inc(S["x_high"], 1)
                    to_dve = k % 2
                    summed, squared = (S["dve_summed"], S["squared_dve"]) if to_dve else (S["pool_summed"], S["squared_pool"])
                    dest = acc_sq[to_dve] if k < 2 else sq[to_dve]
                    if k >= 4:
                        act.wait_ge(summed, 7 * phase + (k - 4) // 2 + 1)
                    act.activation(dest, h_all[:, k, :], ACT.Square).then_inc(squared, 1)

            def root(phase):
                act.wait_ge(S["stats_ready"], phase + 1)
                act.activation(halves(rstd[:, :]), sc_t, ACT.Sqrt, scale=1.0 / D, bias=eps).then_inc(S["root_ready"], 1)

            act.wait_ge(S["lam_summed"], 1)
            act.activation(lam_e, lam_s, ACT.Exp).then_inc(S["lam_exped"], 1)
            act.wait_ge(S["gains_ready"], 1)

            def x_ready(k):
                if k == 8:
                    high(Slab(0))
                act.wait_ge(S["x_copied"], k + 1)
            norm_split(0, V_MIX, x_ready)
            act.wait_ge(S["x_copied"], KD)
            act.dma_start(h_spill, late).then_inc(S["h_spilled"], 16)
            high(Slab(1))
            root(0)

            def swap(t, pair):
                act.wait_ge(S["acc_ready"], t + 1)
                if not is_first(t):
                    act.wait_ge(S["rotated"], t)
                for n in range(4):
                    o = n + 1 - 2 * (n % 2)
                    ins = act.activation(halves(v_now[32 * n:32 * n + 32, :]), pair[32 * o:32 * o + 32, :, 0:HT], ACT.Copy)
                ins.then_inc(S["swapped"], 1)

            def qk_iteration(j, first=False):
                swap(2 * j, acc[0])
                high(Slab(2, j))
                act.wait_ge(S["mail_ready"], j + 1)
                if not first:
                    act.wait_ge(S["nat_stored"], 16 * j)
                A.says(act.activation(v_nat[:, :], mbank[:, :], ACT.Copy), S["mail_free"], j + 1)
                A.wait()
                act.dma_start(k_prompt[0, 0].rearrange("(b p) c d -> p b (c d)", p=P)[:, :, ds(j * P, P)],
                              v_nat[:, :].rearrange("p (b n) -> p b n", b=4)).then_inc(S["nat_stored"], 16)
                swap(2 * j + 1, acc[1])
                high(Slab(3, j))
            qk_iteration(0, first=True)
            with act.Fori(1, NH) as j:
                qk_iteration(j)

            act.wait_ge(S["snew_ready"], 1)
            act.activation(s_new, obank[0:16, 0:NB], ACT.Copy).then_inc(S["exped"], 1)

            def take(g, e, dest, src, scale=1.0):
                act.wait_ge(S["mail_ready"], mail(g, e) + 1)
                A.says(act.activation(dest, src, ACT.Copy, scale=scale), S["mail_free"], mail(g, e) + 1)

            def exps(g, b):
                act.wait_ge(S["maxed"], 4 * g + b + 1)
                act.wait_ge(S["combined"], 4 * g + b + 1)
                n = (b + 1) * P
                for c in (0, 1):
                    ins = act.activation(probs[:, c, 0:n], sc[:, c, 0:n], ACT.Exp, bias=top[:, c:c + 1],
                                         scale=SCALE, accum_out=esum[:, c:c + 1])
                ins.then_inc(S["exped"], 1)

            def attention(g, fill):
                exps(g, 0)
                act.wait_ge(S["multiplied"], NPG * g + 1)
                take(g, E_QB, qb[:, 0:512], mbank[:, :])
                take(g, E_QB + 1, qb[:, 512:1024], mbank[:, :])
                exps(g, 1)
                take(g, E_TR01, w_turn[0][:, 0:P], mbank[:, 0:P])
                exps(g, 2)
                take(g, E_TR01 + 1, w_turn[1][:, 0:2 * P], mbank[:, 0:2 * P])
                fill(0)
                exps(g, 3)
                act.wait_ge(S["diff_ready"], g + 1)
                act.wait_ge(S["mail_ready"], mail(g, E_SAM) + 1)
                A.says(act.activation(s_row[:, 0:PAST], mbank[0:16, :], ACT.Copy), S["mail_free"], mail(g, E_SAM) + 1)
                act.activation(s_row[:, PAST:PAST + 1], s_new[:, ds(g, 1)], ACT.Copy).then_inc(S["s_ready"], 1)
                act.wait_ge(S["o_ready"], 4 * g + 1)
                take(g, E_TR23, w_turn[0][:, 0:3 * P], mbank[:, 0:3 * P])
                act.wait_ge(S["s_maxed"], g + 1)
                act.activation(e_row, s_row, ACT.Exp, bias=top16, scale=SCALE, accum_out=sum16).then_inc(S["s_exped"], 1)
                act.wait_ge(S["o_ready"], 4 * g + 2)
                take(g, E_TR23 + 1, w_turn[1][:, :], mbank[:, :])
                act.wait_ge(S["mail_ready"], mail(g, E_W) + 1)
                A.step(act.activation(w_past[:, 0:NPG * NH], mbank[:, 0:NPG * NH], ACT.Copy))
                A.says(act.activation(w_new[:, ds(g, 1), :], mbank[:, NPG * NH:(NPG + 1) * NH].rearrange("p (a h) -> p a h", a=1),
                                      ACT.Copy), S["mail_free"], mail(g, E_W) + 1)
                act.wait_ge(S["o_ready"], 4 * g + 4)
                for b in range(4):
                    ins = act.activation(probs[:, 0, b * P:(b + 1) * P],
                                         obank[:, b * P:(b + 1) * P], ACT.Square, accum_out=o_ss[:, b:b + 1])
                A.step(ins)
                A.wait()
                act.activation(o_root, o_ss, ACT.Sqrt, scale=1.0 / P, bias=eps).then_inc(S["o_squared"], 1)
                take(g, E_PV, w_turn[0][0:NH, :], mbank[0:NH, :])
                fill(1)
                take(g, E_PV + 1, w_turn[1][0:NH, :], mbank[0:NH, :])
                take(g, E_OT, q_all[:, ds(g, 1), 0:SEQ], mbank[:, :].rearrange("p (a n) -> p a n", a=1), scale=gsub)
                act.wait_ge(S["mail_ready"], mail(g, E_PT) + 1)
                own = mbank[:, 0:(NH - 1) * (NH + 1) + 1:NH + 1]
                A.says(act.activation(o_new[:, ds(g, 1), :], own.rearrange("p (a h) -> p a h", a=1), ACT.Copy),
                       S["mail_free"], mail(g, E_PT) + 1)

            def v_natural(h, first=False):
                act.wait_ge(S["mail_ready"], mail(h - 1, E_VN) + 1)
                if not first:
                    act.wait_ge(S["v_stored"], 16 * h)
                A.says(act.activation(v_nat[:, :], mbank[:, :], ACT.Copy), S["mail_free"], mail(h - 1, E_VN) + 1)
                A.wait()
                act.dma_start(v_prompt[0, 0].rearrange("(b p) c d -> p b (c d)", p=P)[:, :, ds(h * P, P)],
                              v_nat[:, :].rearrange("p (b n) -> p b n", b=4)).then_inc(S["v_stored"], 16)

            def vu_fill(h):
                def fill(s):
                    act.wait_ge(S["acc_ready"], VU_N + s + 2 * h + 1)
                    high(Slab(VU_N + 2 + s, h))
                return fill
            act.wait_ge(S["nat_stored"], 16 * NH)
            act.wait_ge(S["h_spilled"], 16)
            vu_fill(0)(0)
            vu_fill(0)(1)
            v_natural(0, first=True)
            for h in A.loop(1, NH, 2):
                attention(h - 1, vu_fill(h))
                v_natural(h)
            attention(NH - 1, lambda s: None)

            act.wait_ge(S["naturals"], 1)
            act.activation(nat_k[0:NB, :].rearrange("p (a n) -> p a n", a=2), sc[0:NB, :, :], ACT.Copy).then_inc(S["naturals_copied"], 1)
            act.wait_ge(S["naturals"], 2)
            act.activation(nat_v[0:NB, :].rearrange("p (a n) -> p a n", a=2), acc[0][0:NB, :, :], ACT.Copy).then_inc(S["naturals_copied"], 1)
            act.wait_ge(S["naturals"], 3)
            act.activation(nat_u[0:23, :].rearrange("p (a n) -> p a n", a=2), acc[1][0:23, :, :], ACT.Copy).then_inc(S["naturals_copied"], 1)
            act.wait_ge(S["naturals_copied"], 3)
            act.dma_start(k_sample[0].rearrange("b s c d -> (b s) (c d)"), nat_k[0:NB, :]).then_inc(S["naturals_stored"], 16)
            act.dma_start(v_sample[0].rearrange("b s c d -> (b s) (c d)"), nat_v[0:NB, :]).then_inc(S["naturals_stored"], 16)
            act.dma_start(pool_prompt[0, 0], nat_u[0:PS, :]).then_inc(S["naturals_stored"], 16)
            act.dma_start(pool_sample[0, :, PS - 1, :], nat_u[PS:PS + NB, :]).then_inc(S["naturals_stored"], 16)
            act.wait_ge(S["onew_stats"], 1)
            act.activation(v_squares[:, 64:128], obank[:, 0:64], ACT.Sqrt, scale=1.0 / P, bias=eps).then_inc(S["onew_root"], 1)

            def pooled_high(g):
                if g == 0:
                    act.wait_ge(S["u_taken"], 2 * NH)
                if g >= 2:
                    act.wait_ge(S["acc_ready"], POOL_T + 2 * (g - 1))
                for k in (0, 1):
                    act.activation(act_h[:, 2 * (g % 2) + k, :], k_all[:, 2 * g + k, :], ACT.Copy).then_inc(S["pooled_high"], 1)

            def o_high(g):
                for k in (2 * g, 2 * g + 1):
                    act.activation(xh[:, k, :], q_all[:, k, :], ACT.Copy).then_inc(S["x_high"], 1)

            def pool_out_high(g):
                for t in (2 * g, 2 * g + 1):
                    act.wait_ge(S["acc_ready"], POOL_T + t + 1)
                    act.activation(halves(xh[:, NH + t, :]), out(t), ACT.Copy,
                                   scale=gains[:, V_POOL + t:V_POOL + t + 1]).then_inc(S["pool_high"], 1)
            act.wait_ge(S["onew_done"], 1)
            act.wait_ge(S["v_stored"], 16 * NH)
            pooled_high(0)
            for g in range(4):
                if g + 1 < 4:
                    pooled_high(g + 1)
                o_high(g)
                pool_out_high(g)
            high(Slab(POOL_N + 2))

            def after(t, slab):
                act.wait_ge(S["acc_ready"], t + 1)
                high(slab)
            with act.Fori(0, KD // 2) as j:
                after(OUT_T + 2 * j, Slab(OUT_N + 2, j))
                after(OUT_T + 1 + 2 * j, Slab(OUT_N + 3, j))

            norm_split(1, V_FFN, lambda k: act.wait_ge(S["acc_free"], OUT_T + k + 1))
            root(1)

            def gate_up(c, j):
                n = FFN_N, c * (FFN_STEP // 2) + j
                number = c * CH + j
                act.wait_ge(S["acc_free"], FFN_T + c * FFN_TSTEP + 2 * j + 1)
                act.activation(silu_row[0], gate_row[0], ACT.Silu).then_inc(S["silued"], 1)
                high(Slab(n[0] + 2, n[1]))
                act.wait_ge(S["act_product"], number + 1)
                act.activation(act_h[:, ds(j, 1), :], act_row.rearrange("p (a t) -> p a t", a=1), ACT.Copy).then_inc(S["act_high_done"], 1)
                high(Slab(n[0] + 3, n[1]))

            def down(c, i):
                for s in (0, 1):
                    after(FFN_T + 2 * CH + 4 * s + 3 + c * FFN_TSTEP + 8 * i,
                          Slab(FFN_N + 2 * CH + s + 2, c * (FFN_STEP // 2) + i))
            with act.Fori(0, NCH) as c:
                with act.Fori(0, CH) as j:
                    gate_up(c, j)
                with act.Fori(0, CH // 2) as i:
                    down(c, i)

            def wp(j):
                act.wait_ge(S["wp_landed"], 16 * (j + 1))
                if not is_first(j):
                    act.wait_ge(S["proj_ready"], 2 * j)
                act.activation(act_h[:, 2, 0:512], wp_raw, ACT.Copy).then_inc(S["wp_high"], 1)

            for k in (0, 1):
                act.activation(act_h[:, k, :], p_turn[:, k, :], ACT.Copy).then_inc(S["p_high"], 1)
            norm_split(2, V_PLE, lambda k: act.wait_ge(S["acc_free"], PLE_T - KD + k + 1))
            root(2)
            wp(0)

            def ple(j, more=True):
                for s in (0, 1):
                    m = 2 * j + s
                    act.wait_ge(S["acc_free"], PLE_T + m + 1)
                    act.activation(silu_row[s], gate_row[s], ACT.Sigmoid).then_inc(S["silued"], 1)
                    if more:
                        high(Slab(PLE_N + s + 2, j))
                    act.wait_ge(S["pool_summed"], 7 * 3 + m)
                    act.wait_ge(S["h_done"], m + 1)
                    act.activation(hg_row[s], h_all[:, ds(m, 1), :].rearrange("p a t -> p (a t)"), ACT.Copy,
                                   scale=gains[:, ds(m + V_FINAL, 1)]).then_inc(S["hg_ready"], 1)
                    A.says(act.activation(sq[0], h_all[:, ds(m, 1), :].rearrange("p a t -> p (a t)"), ACT.Square),
                           S["squared"], m + 1)
                    if s == 1 and more:
                        wp(j + 1)
                    A.wait()
                    act.wait_ge(S["y_turned"], m + 1)
                    act.activation(ys_nat[:, ds(m * P, P)], obank[0:NB, 0:P], ACT.Copy)
                    act.activation(h_all[:, ds(m, 1), 0:SEQ], mbank[:, :].rearrange("p (a n) -> p a n", a=1),
                                   ACT.Copy).then_inc(S["y_taken"], 1)
            with act.Fori(0, KD // 2 - 1) as j:
                ple(j)
            ple(KD // 2 - 1, more=False)

            act.wait_ge(S["fin_stats"], 1)
            act.activation(fin[:, 0:4], sc[:, 0, 0:4], ACT.Sqrt, scale=1.0 / D, bias=eps).then_inc(S["fin_root"], 1)
            act.activation(fin[0:NB, 4:5], sc[0:NB, 0, 4:5], ACT.Sqrt, scale=1.0 / D, bias=eps[0:NB, :]).then_inc(S["fin_root"], 1)
            act.wait_ge(S["fin_inv"], 2)
            act.wait_ge(S["y_taken"], KD)

            def store(b):
                act.dma_start(y_prompt[0, b * P:(b + 1) * P, :].rearrange("p (k n) -> p k n", n=P),
                              h_all[:, :, b * P:(b + 1) * P]).then_inc(S["y_stored"], 16)
            for b in (0, 1):
                blk = h_all[:, :, b * P:(b + 1) * P]
                A.step(act.activation(blk, blk, ACT.Copy, scale=fin[:, 8 + b:9 + b]))
                A.wait()
                store(b)
            for b in (2, 3):
                act.wait_ge(S["y_scaled"], b - 1)
                store(b)
            act.wait_ge(S["y_scaled"], 3)
            act.dma_start(y_sample.rearrange("b s n -> (b s) n"), ys_nat).then_inc(S["y_stored"], 16)

        @block.vector
        def _(dve):
            V = Steps(dve, S["dve_step"])
            tt, stt, ts = dve.tensor_tensor, dve.scalar_tensor_tensor, dve.tensor_scalar

            def low(slab):
                dve.wait_ge(S["w_high_done"], slab.index + 1)
                tt(wl[slab.slot][:, :], raw[slab.slot][:, :], wh[slab.slot][:, :].bitcast(F32),
                   ALU.subtract).then_inc(S["w_low_done"], 1)

            def x_low(k, src, scalar, base):
                dve.wait_ge(S["x_high"], base + k + 1)
                if scalar is None:
                    ins = tt(xl[:, k, :], src, xh[:, k, :].bitcast(F32), ALU.subtract)
                else:
                    ins = stt(out=xl[:, k, :], in0=src, scalar=scalar, in1=xh[:, k, :].bitcast(F32),
                              op0=ALU.mult, op1=ALU.subtract)
                ins.then_inc(S["x_low"], 1)

            def norm_split(phase, gain, base, k):
                x_low(k, h_all[:, k, :], gains[:, gain + k:gain + k + 1], base)
                if k % 2 and k > 1:
                    dve.wait_ge(S["squared_dve"], 8 * phase + k // 2 + 1)
                    if k > 3:
                        dve.wait_ge(S["dve_summed"], 7 * phase + k // 2 - 1)
                    tt(acc_sq[1], acc_sq[1], sq[1], ALU.add).then_inc(S["dve_summed"], 1)

            def invert_root(phase):
                dve.wait_ge(S["root_ready"], phase + 1)
                V.step(dve.reciprocal(rstd[:, :], rstd[:, :]))

            dve.wait_ge(S["gains_landed"], 16 * 11)
            V.step(tt(lam_pr, lam_in[:, 0:4:2, :], lam_in[:, 1:4:2, :], ALU.mult))
            V.wait()
            dve.tensor_reduce(lam_s, lam_pr, AX.X, ALU.add).then_inc(S["lam_summed"], 1)
            dve.wait_ge(S["setup_turned"], 1)
            V.step(dve.tensor_copy(h_all[:, :, SEQ:T], mbank[:, 0:KD * NB].rearrange("p (k b) -> p k b", k=KD)))
            dve.wait_ge(S["setup_turned"], 2)
            V.says(dve.tensor_copy(gains[:, :], obank[:, 0:V_ALL]), S["gains_ready"], 1)
            V.wait()
            V.step(ts(gsub, gains[:, V_SUB:V_SUB + 1], 1.0 - LAM0, None, ALU.mult))
            dve.wait_ge(S["lam_exped"], 1)
            V.step(tt(lam_d, lam_e[:, 1:2], lam_e[:, 0:1], ALU.subtract))
            V.wait()
            ts(lam_d, lam_d, -LAM0, None, ALU.add).then_inc(S["lam_ready"], 1)
            for k in range(KD):
                dve.wait_ge(S["x_turned"], k + 1)
                dve.tensor_copy(h_all[:, k, 0:SEQ], sc[:, k % 2, :]).then_inc(S["x_copied"], 1)
                if k == 9:
                    low(Slab(0))
                if k >= 1:
                    norm_split(0, V_MIX, 0, k - 1)
            norm_split(0, V_MIX, 0, KD - 1)
            dve.wait_ge(S["state_summed"], 1)
            dve.tensor_copy(state_sum, obank[:, 0:PT * NB]).then_inc(S["state_ready"], 1)
            low(Slab(1))
            dve.wait_ge(S["neglam_summed"], 1)
            V.says(dve.tensor_copy(neglam[:, :], obank[:, 0:1]), S["neglam_ready"], 1)
            V.wait()
            V.step(ts(sgnlam, C[0:16, C_SGN + 1:C_SGN + 2], neglam[0:16, :], C[0:16, C_SGN:C_SGN + 1], ALU.mult, ALU.add))
            invert_root(0)
            V.wait()
            dve.wait_ge(S["rope_landed"], 32)
            V.step(tt(cos_r, q_now[:, :], rstd[:, :], ALU.mult))
            V.step(tt(sin_r, nat[:, :], rstd[:, :], ALU.mult))
            V.wait()

            def rotate(t, pair, dest):
                dve.wait_ge(S["swapped"], t + 1)
                V.says(tt(halves(cos_part), pair[:, :, 0:HT], halves(cos_r), ALU.mult), S["acc_free"], t + 1)
                V.step(tt(v_now[:, :], v_now[:, :], sin_r, ALU.mult))
                V.wait()
                tt(dest, cos_part, v_now[:, :], ALU.add).then_inc(S["rotated"], 1)
            cos_part = q_now[:, :]

            def qk_iteration(j, first=False):
                if not first:
                    dve.wait_ge(S["k_stored"], j)
                    dve.wait_ge(S["mail_ready"], j)
                rotate(2 * j, acc[0], k_now[:, :])
                low(Slab(2, j))
                rotate(2 * j + 1, acc[1], q_all[:, ds(j, 1), :].rearrange("p a t -> p (a t)"))
                low(Slab(3, j))
            V.wait()
            saved = V.k
            qk_iteration(0, first=True)
            per = V.k - saved
            for j in V.loop(1, NH, per):
                qk_iteration(j)

            dve.wait_ge(S["rotated"], 2 * NH)
            dve.wait_ge(S["k_stored"], NH)
            V.step(dve.tensor_copy(k_new, k_all[:, :, SEQ:T]))
            V.says(dve.tensor_copy(q_new, q_all[:, :, SEQ:T]), S["new_taken"], 1)
            V.step(dve.memset(prod_new, 0.0))
            V.wait()
            pn = prod_new.rearrange("p (b h c) -> p h b c", b=NB, c=2)
            V.step(tt(pn[0:HD, :, :, 0], q_all[0:HD, :, SEQ:T], k_all[0:HD, :, SEQ:T], ALU.mult))
            tt(pn[HD:P, :, :, 1], q_all[HD:P, :, SEQ:T], k_all[HD:P, :, SEQ:T], ALU.mult).then_inc(S["new_products"], 1)
            dve.memset(u_row[1][:, 0:16], 0.0).then_inc(S["combined"], 1)
            dve.memset(u_row[2][:, 0:16], 0.0).then_inc(S["o_scaled"], 1)
            V.says(dve.memset(u_row[0][:, 0:16], 0.0), S["diff_ready"], 1)
            V.wait()

            def soften(g, b):
                dve.wait_ge(S["scored"], 4 * g + b + 1)
                n = b * P
                mask = C[:, C_MASK:C_MASK + P].rearrange("p (a n) -> p a n", a=1).to_broadcast([P, 2, P])
                V.step(tt(sc[:, :, n:n + P], sc[:, :, n:n + P], mask, ALU.add))
                V.wait()
                V.step(dve.tensor_reduce(einv, sc[:, :, 0:n + P], AX.X, ALU.max))
                V.wait()
                ts(top, einv, -SCALE, None, ALU.mult).then_inc(S["maxed"], 1)

            def combine(g, b, e):
                n = (b + 1) * P
                dve.wait_ge(S["exped"], 4 * g + b + 2)
                V.step(dve.reciprocal(einv, esum))
                V.wait()
                V.step(ts(probs[:, 1, 0:n], probs[:, 1, 0:n], einv[:, 1:2], neglam[:, :], ALU.mult, ALU.mult))
                V.wait()
                dve.wait_ge(S["mail_ready"], mail(g, e) + 1)
                stt(out=w_row[:, 0:n], in0=probs[:, 0, 0:n], scalar=einv[:, 0:1], in1=probs[:, 1, 0:n],
                    op0=ALU.mult, op1=ALU.add).then_inc(S["combined"], 1)

            def dots(g, ps_):
                for n in ps_:
                    dve.wait_ge(S["multiplied"], NPG * g + n + 2)
                    dve.tensor_reduce(s_past[:, n, :], pages[:, n, :].rearrange("p (h d) -> p h d", d=HD), AX.X,
                                      ALU.add).then_inc(S["dotted"], 1)

            def take_v(h, first=False):
                dve.wait_ge(S["acc_ready"], VU_N + 2 * h + 1)
                if not first:
                    dve.wait_ge(S["mail_ready"], mail(h - 2, E_VN) + 1)
                V.says(tt(halves(v_now[:, :]), acc[0][:, :, 0:HT], halves(rstd[:, :]), ALU.mult), S["acc_free"], VU_N + 2 * h + 1)
                V.wait()
                dve.tensor_copy(v_new[:, ds(h, 1), :], v_now[:, SEQ:T].rearrange("p (a b) -> p a b", a=1)).then_inc(S["v_ready"], 1)

            def take_u(h):
                u, a, b = u_row
                dve.wait_ge(S["acc_ready"], VU_N + 2 * h + 2)
                V.says(tt(halves(u[:, 16:16 + T]), acc[1][:, :, 0:HT], halves(rstd[:, :]), ALU.mult), S["acc_free"], VU_N + 2 * h + 2)
                V.wait()
                col = [C[:, ds(4 * h + C_WIN + i, 1)] for i in range(4)]
                dve.tensor_copy(u_new[:, ds(h, 1), :], u[:, 16 + SEQ - PS:16 + T].rearrange("p (a b) -> p a b", a=1)).then_inc(S["u_taken"], 1)
                V.step(tt(a[:, 16:528], u[:, 16:528], u[:, 15:527], ALU.add))
                V.wait()
                V.step(stt(out=b[:, 16:528], in0=a[:, 14:526], scalar=col[0], in1=a[:, 16:528], op0=ALU.mult, op1=ALU.add))
                V.wait()
                V.step(stt(out=a[:, 16:528], in0=b[:, 12:524], scalar=col[1], in1=b[:, 16:528], op0=ALU.mult, op1=ALU.add))
                V.wait()
                V.step(stt(out=b[:, 16:528], in0=a[:, 8:520], scalar=col[2], in1=a[:, 16:528], op0=ALU.mult, op1=ALU.add))
                V.step(tt(b[:, 528:536], u[:, 528:536], state_sum[:, ds(h * NB, NB)], ALU.add))
                V.wait()
                V.step(tt(a[:, 16:32], b[:, 16:32], C[:, ds(h * 16 + C_INV, 16)], ALU.mult))
                V.wait()
                dve.wait_ge(S["staged"], h + 1)
                dest = k_all[:, ds(h, 1), :].rearrange("p a t -> p (a t)")
                V.step(tt(dest[:, 0:16], a[:, 16:32], u[:, 16:32], ALU.subtract))
                stt(out=dest[:, 16:T], in0=b[:, 32:536], scalar=col[3], in1=u[:, 32:536], op0=ALU.mult,
                    op1=ALU.subtract).then_inc(S["u_taken"], 1)

            def sample_max(g):
                dve.wait_ge(S["s_ready"], g + 1)
                V.step(dve.tensor_reduce(inv16, s_row, AX.X, ALU.max))
                V.wait()
                ts(top16, inv16, -SCALE, None, ALU.mult).then_inc(S["s_maxed"], 1)

            def sample_diff(g):
                dve.wait_ge(S["s_exped"], g + 1)
                V.step(dve.reciprocal(inv16, sum16))
                V.wait()
                V.step(tt(inv16, inv16, sgnlam, ALU.mult))
                V.wait()
                dve.wait_ge(S["mail_ready"], mail(g - 1, E_W) + 1)
                V.step(ts(diff16, C[0:16, C_PAIR:C_PAIR + NH], inv16, None, ALU.mult))
                V.wait()
                ts(diff16n, diff16, e_row[:, PAST:PAST + 1], None, ALU.mult).then_inc(S["diff_ready"], 1)

            def scale_o(g):
                dve.wait_ge(S["o_squared"], g + 1)
                V.step(dve.reciprocal(o_inv, o_root))
                V.wait()
                dve.wait_ge(S["mail_ready"], mail(g - 1, E_OT) + 1)
                tt(nat[:, 0:SEQ].rearrange("p (b e) -> p b e", b=4), obank[:, :].rearrange("p (b e) -> p b e", b=4),
                   o_inv.rearrange("p (b a) -> p b a", a=1).to_broadcast([P, 4, P]), ALU.mult).then_inc(S["o_scaled"], 1)

            def attention(g, fill_v, fill_u):
                soften(g, 0)
                combine(g, 0, E_TR23 + 1 - EV)
                soften(g, 1)
                combine(g, 1, E_TR01)
                dots(g, (0,))
                soften(g, 2)
                dots(g, (1,))
                combine(g, 2, E_TR01 + 1)
                dots(g, (2, 3))
                soften(g, 3)
                fill_v()
                combine(g, 3, E_TR23)
                sample_max(g)
                sample_diff(g)
                scale_o(g)
                fill_u()

            def fills(h, first=False):
                def v():
                    take_v(h, first)
                    low(Slab(VU_N + 2, h))

                def u():
                    take_u(h)
                    low(Slab(VU_N + 3, h))
                return v, u
            v, u = fills(0, first=True)
            v()
            u()
            STEPS_VU = 4 * 4 + 1 + 3 + 1 + 7
            for h in V.loop(1, NH, STEPS_VU):
                attention(h - 1, *fills(h))
            attention(NH - 1, lambda: None, lambda: None)

            dve.wait_ge(S["mail_free"], mail(NH - 1, E_PT) + 1)
            w_hb = w_new.rearrange("p b h -> p h b")
            o_hb = o_new.rearrange("p b h -> p h b")
            V.step(tt(prod_new[:, 0:64].rearrange("p (h b) -> p h b", h=NH), w_hb, v_new, ALU.mult))
            V.wait()
            V.step(tt(prod_new[:, 64:128].rearrange("p (h b) -> p h b", h=NH), o_hb,
                      prod_new[:, 0:64].rearrange("p (h b) -> p h b", h=NH), ALU.add))
            V.wait()
            tt(v_squares[:, 0:64], prod_new[:, 64:128], prod_new[:, 64:128], ALU.mult).then_inc(S["onew_squared"], 1)
            dve.wait_ge(S["onew_root"], 1)
            V.step(dve.reciprocal(v_squares[:, 0:64], v_squares[:, 64:128]))
            V.wait()
            stt(out=q_all[:, :, SEQ:T], in0=prod_new[:, 64:128].rearrange("p (h b) -> p h b", h=NH), scalar=gsub,
                in1=v_squares[:, 0:64].rearrange("p (h b) -> p h b", h=NH), op0=ALU.mult,
                op1=ALU.mult).then_inc(S["onew_done"], 1)

            def pooled_low(g):
                for k in (0, 1):
                    dve.wait_ge(S["pooled_high"], 2 * g + k + 1)
                    tt(act_l[:, 2 * (g % 2) + k, :], k_all[:, 2 * g + k, :], act_h[:, 2 * (g % 2) + k, :].bitcast(F32),
                       ALU.subtract).then_inc(S["pooled_low"], 1)
            pooled_low(0)
            for g in range(4):
                if g + 1 < 4:
                    pooled_low(g + 1)
                for k in (2 * g, 2 * g + 1):
                    x_low(k, q_all[:, k, :], None, KD)
                for t in (2 * g, 2 * g + 1):
                    dve.wait_ge(S["pool_high"], t + 1)
                    stt(out=halves(xl[:, NH + t, :]), in0=out(t), scalar=gains[:, V_POOL + t:V_POOL + t + 1],
                        in1=halves(xh[:, NH + t, :].bitcast(F32)), op0=ALU.mult,
                        op1=ALU.subtract).then_inc(S["acc_free"], 1)
            low(Slab(POOL_N + 2))

            def add_h(t, pair, m):
                dve.wait_ge(S["acc_ready"], t + 1)
                tile = halves(h_all[:, ds(m, 1), :].rearrange("p a t -> p (a t)"))
                tt(tile, pair[:, :, 0:HT], tile, ALU.add).then_inc(S["acc_free"], 1)

            dve.wait_ge(S["h_loaded"], 32)
            with dve.Fori(0, KD // 2) as j:
                for s in (0, 1):
                    add_h(OUT_T + s + 2 * j, acc[s], 2 * j + s)
                    low(Slab(OUT_N + s + 2, j))

            for k in range(KD):
                norm_split(1, V_FFN, KD + NH, k)
            dve.wait_ge(S["p_turned"], 1)
            V.step(dve.tensor_copy(p_turn[:, 0, 0:SEQ], mbank[:, :]))
            V.step(dve.tensor_copy(p_turn[:, 1, 0:SEQ], obank[:, :]))
            dve.tensor_copy(p_turn[:, :, SEQ:T], sc[:, 0, 0:2 * NB].rearrange("p (k b) -> p k b", k=2)).then_inc(S["p_copied"], 1)
            invert_root(1)
            V.wait()

            def gate_up(c, j):
                t = FFN_T + c * FFN_TSTEP + 2 * j
                number = c * CH + j
                dve.wait_ge(S["acc_ready"], t + 1)
                V.says(tt(halves(gate_row[0]), acc[0][:, :, 0:HT], halves(rstd[:, :]), ALU.mult), S["acc_free"], t + 1)
                low(Slab(FFN_N + 2, c * (FFN_STEP // 2) + j))
                dve.wait_ge(S["acc_ready"], t + 2)
                V.says(tt(halves(up_row), acc[1][:, :, 0:HT], halves(rstd[:, :]), ALU.mult), S["acc_free"], t + 2)
                V.wait()
                dve.wait_ge(S["silued"], number + 1)
                V.says(tt(act_row, up_row, silu_row[0], ALU.mult), S["act_product"], number + 1)
                V.wait()
                dve.wait_ge(S["act_high_done"], number + 1)
                tt(act_l[:, ds(j, 1), :], act_row.rearrange("p (a t) -> p a t", a=1), act_h[:, ds(j, 1), :].bitcast(F32),
                   ALU.subtract).then_inc(S["act_low_done"], 1)
                low(Slab(FFN_N + 3, c * (FFN_STEP // 2) + j))

            def down(c, i):
                for s in (0, 1):
                    for m in range(4):
                        add_h(FFN_T + 2 * CH + 4 * s + m + c * FFN_TSTEP + 8 * i, acc[m % 2], 8 * i + 4 * s + m)
                    low(Slab(FFN_N + 2 * CH + s + 2, c * (FFN_STEP // 2) + i))
            with dve.Fori(0, NCH) as c:
                with dve.Fori(0, CH) as j:
                    gate_up(c, j)
                with dve.Fori(0, CH // 2) as i:
                    down(c, i)

            def wp_low(j):
                dve.wait_ge(S["wp_high"], j + 1)
                tt(act_l[:, 2, 0:512], wp_raw, act_h[:, 2, 0:512].bitcast(F32), ALU.subtract).then_inc(S["wp_low"], 1)
            for k in (0, 1):
                dve.wait_ge(S["p_high"], k + 1)
                tt(act_l[:, k, :], p_turn[:, k, :], act_h[:, k, :].bitcast(F32), ALU.subtract).then_inc(S["p_low"], 1)
            for k in range(KD):
                norm_split(2, V_PLE, 2 * KD + NH, k)
            invert_root(2)
            V.wait()
            wp_low(0)

            def ple(j, more=True):
                for s in (0, 1):
                    m = 2 * j + s
                    t = PLE_T + s + 2 * j
                    dve.wait_ge(S["acc_ready"], t + 1)
                    V.says(tt(halves(gate_row[s]), acc[s][:, :, 0:HT], halves(rstd[:, :]), ALU.mult), S["acc_free"], t + 1)
                    dve.wait_ge(S["proj_ready"], m + 1)
                    dve.wait_ge(S["silued"], NCH * CH + m + 1)
                    V.says(tt(halves(up_row), sc_t, halves(silu_row[s]), ALU.mult), S["proj_free"], m + 1)
                    V.wait()
                    tile = h_all[:, ds(m, 1), :].rearrange("p a t -> p (a t)")
                    tt(tile, tile, up_row, ALU.add).then_inc(S["h_done"], 1)
                    if more:
                        low(Slab(PLE_N + s + 2, j))
                    if s == 1 and more:
                        wp_low(j + 1)
            with dve.Fori(0, KD // 2 - 1) as j:
                ple(j)
            ple(KD // 2 - 1, more=False)
            dve.wait_ge(S["fin_root"], 2)
            dve.reciprocal(fin[:, 8:12], fin[:, 0:4]).then_inc(S["fin_inv"], 1)
            dve.reciprocal(fin[0:NB, 12:13], fin[0:NB, 4:5]).then_inc(S["fin_inv"], 1)
            dve.wait_ge(S["fin_inv"], 2)
            dve.wait_ge(S["y_taken"], KD)
            for b in (2, 3):
                blk = h_all[:, :, b * P:(b + 1) * P]
                ts(blk, blk, fin[:, 8 + b:9 + b], None, ALU.mult).then_inc(S["y_scaled"], 1)
            ts(ys_nat, ys_nat, fin[0:NB, 12:13], None, ALU.mult).then_inc(S["y_scaled"], 1)

        @block.gpsimd
        def _(pool):
            def copy(o, i):
                return pool.tensor_copy(o, i)

            def add_squares(phase):
                for k in range(2, KD, 2):
                    pool.wait_ge(S["squared_pool"], 8 * phase + k // 2 + 1)
                    if k > 2:
                        pool.wait_ge(S["pool_summed"], 7 * phase + k // 2 - 1)
                    pool.tensor_tensor(acc_sq[0], acc_sq[0], sq[0], ALU.add).then_inc(S["pool_summed"], 1)
            add_squares(0)
            with pool.Fori(0, NH) as j:
                pool.wait_ge(S["rotated"], 2 * j + 1)
                copy(k_all[:, ds(j, 1), :].rearrange("p a t -> p (a t)"), k_now[:, :]).then_inc(S["k_stored"], 1)

            def stage(h):
                copy(q_now[:, :], q_all[:, ds(h, 1), :].rearrange("p a t -> p (a t)"))
                copy(k_now[:, :], k_all[:, ds(h, 1), :].rearrange("p a t -> p (a t)")).then_inc(S["staged"], 1)

            def query(b):
                copy(q_col.rearrange("p (h a) -> p h a", a=1), q_new[:, :, ds(b, 1)]).then_inc(S["qcol_ready"], 1)

            def multiply(g):
                pool.wait_ge(S["mail_free"], mail(g, E_QB + 1) + 1)
                for n in range(NPG):
                    pool.wait_ge(k_landed[n], 16 * (g + 1))
                    pool.tensor_tensor(pages[:, n, :], pages[:, n, :], qb, ALU.mult).then_inc(S["multiplied"], 1)
            pool.wait_ge(S["rotated"], 2 * NH)
            pool.wait_ge(S["k_stored"], NH)
            pool.wait_ge(S["mail_ready"], NH)
            pool.wait_ge(S["new_taken"], 1)
            query(0)
            copy(q_now[:, :], q_all[:, 0, :]).then_inc(S["multiplied"], 1)
            copy(k_now[:, :], k_all[:, 0, :]).then_inc(S["staged"], 1)
            with pool.Fori(1, NH) as h:
                multiply(h - 1)
                query(h)
                pool.wait_ge(S["scored"], 4 * h)
                stage(h)
            multiply(NH - 1)
            for phase in (1, 2):
                if phase == 1:
                    pool.wait_ge(S["x_low"], KD + NH)
                add_squares(phase)
            pool.wait_ge(S["stats_ready"], 3)
            pool.memset(acc_sq[0], 0.0).then_inc(S["pool_step"], 1)
            pool.wait_ge(S["pool_step"], 1)
            with pool.Fori(0, KD) as m:
                pool.wait_ge(S["squared"], m + 1)
                pool.wait_ge(S["pool_summed"], m + 7 * 3)
                pool.tensor_tensor(acc_sq[0], acc_sq[0], sq[0], ALU.add).then_inc(S["pool_summed"], 1)


_INS = ["x_prompt", "x_sample", "p_prompt", "p_sample", "cache_k", "cache_v", "state_pool", "page_table",
        "g_mix", "w_in", "w_out", "lambda_q1", "lambda_k1", "lambda_q2", "lambda_k2", "g_sub", "w_pool",
        "pool_scale", "g_ffn", "w_gate_up", "w_down", "g_ple", "w_ple_gate", "w_ple_proj", "g_final"]
_OUTS = [(1, SEQ, D), (NB, 1, D), (1, 1, SEQ, 2 * NH, HD), (1, 1, SEQ, NH, P), (1, 1, PS, PW),
         (1, NB, 1, 2 * NH, HD), (1, NB, 1, NH, P), (1, NB, PS, PW)]


def kernel(**inputs):
    import concourse.bacc as bacc
    from concourse.bass_utils import run_bass_kernel_spmd as run

    nc = bacc.Bacc("TRN2", target_bir_lowering=False, num_devices=1)
    arrays, args = {}, []
    given = [(n, np.ascontiguousarray(inputs[n])) for n in _INS]
    for name, a in given + [("const", constants()), ("rope", rope_tables())]:
        arrays[f"in_{name}"] = a
        args.append(nc.dram_tensor(f"in_{name}", a.shape, mybir.dt.from_np(a.dtype), kind="ExternalInput").ap())
    for i, shape in enumerate(_OUTS):
        args.append(nc.dram_tensor(f"out_{i}", shape, F32, kind="ExternalOutput").ap())
    layer(nc, *args)
    r = run(nc, [arrays], core_ids=[0])
    return tuple(r.results[0][f"out_{i}"] for i in range(len(_OUTS)))
```

```python
from contextlib import ExitStack

import numpy as np

import concourse.bass as bass
from concourse import mybir

ALU = mybir.AluOpType
ACT = mybir.ActivationFunctionType
AX = mybir.AxisListType
F32 = mybir.dt.float32
F32R = mybir.dt.float32r
I32 = mybir.dt.int32
ds = bass.ds

P = 128
D = 2048
SEQ = 512
NB = 8
T = SEQ + NB
HT = T // 2
KD = D // P
NH = 8
HD = 64
AW = NH * P
PW = D - AW
PT = PW // P
WINDOWS = (2, 4, 8, 16)
PS = max(WINDOWS) - 1
DFF = 5632
PLE = 256
PAST = 512
PAGE = 128
NPG = PAST // PAGE
EPS = 1e-6
LAM0 = 0.8 - 0.6
SCALE = HD ** -0.5
NEG = -1e30
SL = 16 * P
CH = 4
NCH = DFF // P // CH

QKV_N, VU_N = 0, 2 * NH
POOL_N = VU_N + 2 * NH
OUT_N = POOL_N + 1
FFN_N = OUT_N + KD
FFN_STEP = 3 * CH
PLE_N = FFN_N + NCH * FFN_STEP
SLABS = PLE_N + KD
POOL_T = VU_N + 2 * NH
OUT_T = POOL_T + PT
FFN_T = OUT_T + KD
FFN_TSTEP = 2 * CH + KD
PLE_T = FFN_T + NCH * FFN_TSTEP

C_ID, C_MASK, C_ONE, C_INV = 0, 128, 256, 384
C_WIN = C_INV + PT * 16
C_SEL = C_WIN + PT * 4
C_PAIR = C_SEL + len(WINDOWS) * NB
C_SGN = C_PAIR + NH
C_EPS = C_SGN + 2
C_ALL = C_EPS + 1

V_MIX, V_FFN, V_PLE, V_FINAL, V_POOL, V_SUB = 0, 16, 32, 48, 64, 72
V_ALL = 73

EV = 10
MAIL_VU = NH + 1
E_SAM, E_TR0, E_TR1, E_W, E_TR2, E_PV0, E_TR3, E_PV1, E_OT, E_VN = range(EV)
E_TR = (E_TR0, E_TR1, E_TR2, E_TR3)
LEAD = 6
FILLS = 16


def mail(g, e):
    return MAIL_VU + EV * g + e


def constants():
    c = np.zeros((P, C_ALL), np.float32)
    c[:, C_ID:C_ID + P] = np.eye(P, dtype=np.float32)
    c[:, C_MASK:C_MASK + P] = np.where(np.arange(P)[None, :] <= np.arange(P)[:, None], 0.0, NEG)
    c[:, C_ONE:C_ONE + P] = 1.0
    for t in range(PT):
        win = WINDOWS[t * len(WINDOWS) // PT]
        c[:, C_INV + 16 * t:C_INV + 16 * (t + 1)] = 1.0 / np.minimum(np.arange(16) + 1, win)
        c[:, C_WIN + 4 * t:C_WIN + 4 * t + 4] = [win >= 4, win >= 8, win >= 16, 1.0 / win]
    for g, win in enumerate(WINDOWS):
        for b in range(NB):
            c[b * PS + PS - (win - 1):(b + 1) * PS, C_SEL + g * NB + b] = 1.0
    for r in range(2 * NH):
        c[r, C_PAIR + r // 2] = 1.0
        c[r, C_SGN + r % 2] = 1.0
    c[:, C_EPS] = EPS
    return c


def rope_tables():
    half = HD // 2
    inv = np.float32(10000.0) ** (-np.arange(half, dtype=np.float32) / np.float32(half))
    pos = np.concatenate([np.arange(SEQ), np.full(NB, PAST)]).astype(np.float32)
    ang = (inv[:, None] * pos[None, :]).astype(np.float32)
    cos, sin = np.cos(ang), np.sin(ang)
    return np.stack([np.concatenate([cos] * 4), np.concatenate([-sin, sin] * 2)], 1).astype(np.float32)


class Slab:

    def __init__(self, number, half=0):
        self.index = number + 2 * half
        self.slot = number % 2
        self.turn = number // 2 + half


class Steps:

    def __init__(self, eng, sem):
        self.eng, self.sem, self.base, self.k, self.last = eng, sem, 0, 0, None

    def step(self, ins):
        self.k += 1
        ins.then_inc(self.sem, 1)
        self.last = (self.sem, self.base + self.k)

    def says(self, ins, sem, value):
        ins.then_inc(sem, 1)
        self.last = (sem, value)

    def wait(self):
        self.eng.wait_ge(*self.last)

    def loop(self, start, end, per):
        outer = self.base + self.k
        with self.eng.Fori(start, end) as i:
            self.base, self.k = outer + (i - start) * per, 0
            yield i
            assert self.k == per, (self.k, per)
        self.base, self.k = outer + (end - start) * per, 0


def is_first(i):
    return isinstance(i, int) and i == 0


def halves(ap):
    return ap.rearrange("p (a b) -> p a b", a=2)


def layer(nc, x_prompt, x_sample, p_prompt, p_sample, cache_k, cache_v, state_pool, page_table,
          g_mix, w_in, w_out, lq1, lk1, lq2, lk2, g_sub, w_pool, pool_scale, g_ffn, w_gate_up,
          w_down, g_ple, w_ple_gate, w_ple_proj, g_final, const, rope,
          y_prompt, y_sample, k_prompt, v_prompt, pool_prompt, k_sample, v_sample, pool_sample):
    q_rows = nc.dram_tensor("q_rows", (NB, AW), F32, kind="Internal").ap()
    h_spill = nc.dram_tensor("h_spill", (P, KD * T), F32, kind="Internal").ap()
    w_in_v = w_in[0].rearrange("(k p) n -> p k n", p=P)
    w_out_v = w_out[0].rearrange("(k p) n -> p k n", p=P)
    w_gu_v = w_gate_up[0].rearrange("(k p) n -> p k n", p=P)
    w_dn_v = w_down[0].rearrange("(k p) n -> p k n", p=P)
    w_pg_v = w_ple_gate[0].rearrange("(k p) n -> p k n", p=P)
    w_pp_v = w_ple_proj[0].rearrange("(k p) n -> p k n", p=P)
    w_pool_v = w_pool[0].rearrange("g (k p) n -> p (g k) n", p=P)
    k_pages = cache_k[0].rearrange("n t h d -> n t (h d)")
    v_pages = cache_v[0].rearrange("n t h d -> n t (h d)")

    with ExitStack() as ctx:
        def sb(name, shape, dt=F32, where=ctx):
            return where.enter_context(nc.sbuf_tensor(name, shape, dt))

        def ps(name, shape):
            return ctx.enter_context(nc.psum_tensor(name, shape, F32))

        def sem(name):
            return ctx.enter_context(nc.semaphore(name))

        raw = [sb(f"raw{i}", [P, SL]) for i in range(2)]
        wh = [sb(f"w_high{i}", [P, SL], F32R) for i in range(2)]
        wl = [sb(f"w_low{i}", [P, SL], F32R) for i in range(2)]
        xh = sb("x_high", [P, KD, T], F32R)
        xl = sb("x_low", [P, KD, T], F32R)
        rstd = sb("rstd", [P, T])
        sums = sb("sums", [P, 4 * T])
        C = sb("constants", [P, C_ALL])
        gains = sb("gains", [P, V_ALL])
        neglam = sb("neglam", [P, 1])
        region = sb("region", [P, 2 * KD * T])
        keys = sb("key_pages", [P, NPG, AW])
        with ExitStack() as early:
            k_now = sb("k_now", [P, T], where=early)
            q_now = sb("q_now", [P, T], where=early)
            v_now = sb("v_now", [P, T], where=early)
            v_nat = sb("v_nat", [P, SEQ], where=early)
            nat = sb("nat", [P, T], where=early)
            small = sb("small", [P, 1560], where=early)
        act_h = sb("act_high", [P, CH, T], F32R)
        act_l = sb("act_low", [P, CH, T], F32R)

        ident = C[:, C_ID:C_ID + P]
        ones = C[:, C_ONE:C_ONE + P]
        eps = C[:, C_EPS:C_EPS + 1]

        sum_sq = sums[:, 0:T]
        sq = [sums[:, (2 + i) * T:(3 + i) * T] for i in range(2)]
        cos_r, sin_r = sums[:, 0:T], sums[:, T:2 * T]
        u_row = [sums[:, i * (T + 16):(i + 1) * (T + 16)] for i in range(3)]

        q_all = region[:, 0:NH * T].rearrange("p (h t) -> p h t", h=NH)
        k_all = region[:, NH * T:2 * NH * T].rearrange("p (h t) -> p h t", h=NH)
        h_all = region[:, KD * T:2 * KD * T].rearrange("p (k t) -> p k t", k=KD)
        x_nat = [region[:, i * 2048:(i + 1) * 2048].rearrange("p (b n) -> p b n", b=4) for i in range(3)]
        xs_nat = region[0:NB, 3 * 2048:3 * 2048 + D]
        late = region[:, KD * T:]
        pages_v = late[:, 0:NPG * AW].rearrange("p (g n) -> p g n", g=NPG)
        qb = late[:, 4096:5120]
        probs = late[:, 5120:6144].rearrange("p (c k) -> p c k", c=2)
        w_row = late[:, 6144:6656]
        w_turn = [late[:, 6656:7168], small[:, 0:512]]
        s_row = late[0:16, 7168:7168 + PAST + 1]
        e_row = late[0:16, 7700:7700 + PAST + 1]
        state = region[0:NB * PS, 0:PW]
        nat_k, nat_v, nat_u = (keys[:, i, :] for i in range(3))

        def part(start, n):
            return small[:, start:start + n]
        k_new = part(512, 64).rearrange("p (h b) -> p h b", h=NH)
        v_new = part(576, 64).rearrange("p (h b) -> p h b", h=NH)
        q_new = part(640, 64).rearrange("p (h b) -> p h b", h=NH)
        u_new = part(704, NH * 23).rearrange("p (h b) -> p h b", h=NH)
        prod_new = part(888, 128)
        s_new = small[0:16, 1016:1024]
        o_new = part(1024, 64).rearrange("p (b h) -> p b h", b=NB)
        w_new = part(1088, 64).rearrange("p (b h) -> p b h", b=NB)
        state_sum = part(1152, 64)
        s_past = part(1224, 64).rearrange("p (g n) -> p g n", g=NPG)
        w_past = part(1288, 40)
        diff16 = small[0:16, 1328:1336]
        diff16n = small[0:16, 1336:1344]
        sgnlam = small[0:16, 1344:1345]
        top16 = small[0:16, 1345:1346]
        sum16 = small[0:16, 1346:1347]
        inv16 = small[0:16, 1347:1348]
        top = part(1348, 2)
        esum = part(1350, 2)
        einv = part(1352, 2)
        o_ss = part(1354, 4)
        o_inv = part(1358, 4)
        o_root = part(1362, 4)
        gsub = part(1366, 1)
        v_squares = part(1368, 128)

        gate_row = [region[:, i * T:(i + 1) * T] for i in range(2)]
        silu_row = [region[:, (2 + i) * T:(3 + i) * T] for i in range(2)]
        up_row = region[:, 4 * T:5 * T]
        act_row = region[:, 5 * T:6 * T]
        hg_row = [region[:, (6 + i) * T:(7 + i) * T] for i in range(2)]
        ys_nat = region[0:NB, 8 * T:8 * T + D]
        p_nat = region[:, 8 * T + D:8 * T + D + 4 * PLE].rearrange("p (b n) -> p b n", b=4)
        ps_nat = silu_row[0][0:NB, 0:PLE]
        p_turn = region[:, 14 * T:16 * T].rearrange("p (k t) -> p k t", k=2)
        wp_raw = region[:, 8 * T + D:8 * T + D + 4 * P]
        fin = region[:, 8 * T + D + 4 * PLE:8 * T + D + 4 * PLE + 16]
        vec_nat = k_now[0:V_ALL, 0:P]
        lam_in = small[0:1, 0:4 * HD].rearrange("p (a d) -> p a d", a=4)
        lam_pr = small[0:1, 256:256 + 2 * HD].rearrange("p (a d) -> p a d", a=2)
        lam_s = small[0:1, 400:402]
        lam_e = small[0:1, 402:404]
        lam_d = small[0:1, 404:405]
        pt_sb = sb("page_table_sb", [1, NB * NPG], I32)

        acc = [ps(f"acc{i}", [P, 2, 512]) for i in range(2)]
        sc = ps("scores", [P, 2, 512])
        mbank = ps("mail_bank", [P, 512])
        obank = ps("o_bank", [P, 512])
        sc_t = sc[:, :, 0:HT]

        def out(t):
            return acc[t % 2][:, :, 0:HT]

        names = """
            w_low_done o_high_done o_low_done onew_low setup_landed gains_landed rope_landed x_turned state_landed misc_stored
            h_spilled x_low dotted mail_ready naturals_stored onew_done h_loaded
            pooled_low p_landed wp_landed p_copied wp_low nat_stored v_stored y_stored acc_free
            acc_ready pool_summed stats_ready setup_turned x_copied gains_ready
            state_summed state_ready lam_ready neglam_summed rotated mail_free staged root_ready
            exped scored q_stored qb_landed o_new_ready o_new_taken combined o_scaled o_ready diff_ready v_ready new_products
            neglam_ready snew_ready naturals u_taken onew_squared onew_stats naturals_copied
            p_turned act_low_done proj_free proj_ready hg_ready y_taken y_turned p_low fin_stats
            act_step w_high_done x_high lam_summed lam_exped swapped maxed multiplied
            s_ready s_maxed s_exped o_squared onew_root pooled_high pool_high silued act_product
            act_high_done wp_high p_high h_done squared fin_root fin_inv y_scaled dve_step k_stored
            new_taken pool_step""".split()
        S = {n: sem(n) for n in names}
        raw_landed = [sem(f"raw_landed{i}") for i in range(2)]
        x_landed = [sem(f"x_landed{i}") for i in range(4)]
        k_landed = [sem(f"k_page_landed{i}") for i in range(NPG)]
        v_landed = [sem(f"v_page_landed{i}") for i in range(NPG)]

        block = ctx.enter_context(nc.Block())

        def src_qk(j, s):
            return w_in_v[:, :, ds((NH * (1 - s) + j) * P, P)]

        def src_vu(h, s):
            return w_in_v[:, :, ds((NH * (2 + s) + h) * P, P)]

        @block.sync
        def _(sp):
            def load(slab, src, first=False):
                if not first:
                    sp.wait_ge(S["w_low_done"], slab.index - 1)
                k = src.shape[1]
                sp.dma_start(raw[slab.slot][:, :].rearrange("p (k n) -> p k n", k=k), src)\
                    .then_inc(raw_landed[slab.slot], 16)

            def load_pages(b, pages, source, landed, free=()):
                numbers = [sp.value_load(pt_sb[0:1, ds(b * NPG + g, 1)], min_val=0,
                                         max_val=cache_k.shape[1] - 1) for g in range(NPG)]
                if free:
                    sp.wait_ge(*free)
                for g, page in enumerate(numbers):
                    sp.dma_start(pages[:, g, :], source[ds(page, 1), :, :].rearrange("a t n -> t (a n)"))\
                        .then_inc(landed[g], 16)

            xp = x_prompt[0].rearrange("(b p) n -> p b n", p=P)
            sp.dma_start(C[:, :], const).then_inc(S["setup_landed"], 16)
            sp.dma_start(xs_nat, x_sample.rearrange("b s n -> (b s) n")).then_inc(S["setup_landed"], 16)
            sp.dma_start(x_nat[0], xp[:, :, 0:512]).then_inc(x_landed[0], 16)
            for v, at, n in ((g_mix[0], V_MIX, 16), (g_ffn[0], V_FFN, 16), (g_ple[0], V_PLE, 16),
                             (g_final, V_FINAL, 16), (pool_scale[0], V_POOL, 8), (g_sub[0], V_SUB, 1)):
                sp.dma_start(vec_nat[at:at + n, :], v.rearrange("(k p) -> k p", p=P))\
                    .then_inc(S["gains_landed"], 16)
            for i, v in enumerate((lq1, lk1, lq2, lk2)):
                sp.dma_start(lam_in[:, i, :], v).then_inc(S["gains_landed"], 16)
            sp.dma_start(pt_sb[:, :], page_table.rearrange("b n -> (b n)").rearrange("(a n) -> a n", a=1))\
                .then_inc(S["gains_landed"], 16)
            sp.dma_start(x_nat[1], xp[:, :, 512:1024]).then_inc(x_landed[1], 16)
            load(Slab(0), src_qk(0, 0), first=True)
            sp.dma_start(x_nat[2], xp[:, :, 1024:1536]).then_inc(x_landed[2], 16)
            load(Slab(1), src_qk(0, 1), first=True)
            sp.dma_start(q_now[:, :], rope[:, 0, :]).then_inc(S["rope_landed"], 16)
            sp.dma_start(nat[:, :], rope[:, 1, :]).then_inc(S["rope_landed"], 16)
            sp.wait_ge(S["x_turned"], 4)
            sp.dma_start(x_nat[0], xp[:, :, 1536:2048]).then_inc(x_landed[3], 16)
            sp.wait_ge(S["x_turned"], 8)
            sp.dma_start(region[0:NB * PS, 2048:2048 + PW], state_pool[0].rearrange("b s n -> (b s) n"))\
                .then_inc(S["state_landed"], 16)
            sp.dma_start(pool_sample[0, :, 0:PS - 1, :], state_pool[0, :, 1:PS, :])\
                .then_inc(S["misc_stored"], 16)
            sp.wait_ge(S["gains_landed"], 16 * 11)
            load(Slab(2), src_qk(1, 0))
            load(Slab(3), src_qk(1, 1))

            with sp.Fori(2, NH) as j:
                load(Slab(0, j), src_qk(j, 0))
                load(Slab(1, j), src_qk(j, 1))
            load_pages(0, keys, k_pages, k_landed)
            load(Slab(VU_N), src_vu(0, 0))
            load(Slab(VU_N + 1), src_vu(0, 1))

            def load_query(b):
                sp.dma_start(qb, q_rows[ds(b, 1), :].to_broadcast([P, AW])).then_inc(S["qb_landed"], 16)
            sp.wait_ge(S["h_spilled"], 16)
            sp.wait_ge(S["x_low"], KD)
            sp.wait_ge(S["squared"], KD)
            sp.wait_ge(S["q_stored"], 16)
            load_query(0)
            load(Slab(VU_N + 2), src_vu(1, 0))
            load(Slab(VU_N + 3), src_vu(1, 1))
            load_pages(0, pages_v, v_pages, v_landed)

            def vu_iteration(h, loads):
                load_pages(h, keys, k_pages, k_landed, (S["dotted"], NPG * h))
                sp.wait_ge(S["multiplied"], NPG * h)
                load_query(h)
                load(*loads[0])
                load(*loads[1])
                load_pages(h, pages_v, v_pages, v_landed, (S["mail_ready"], mail(h - 1, E_PV1) + 1))

            with sp.Fori(1, NH - 1) as h:
                vu_iteration(h, [(Slab(VU_N + 2 + s, h), src_vu(h + 1, s)) for s in (0, 1)])
            vu_iteration(NH - 1, [(Slab(POOL_N), w_pool_v), (Slab(OUT_N), w_out_v[:, :, 0:P])])

            def src_out(m):
                return w_out_v[:, :, ds(m * P, P)]
            load(Slab(OUT_N + 1), src_out(1))
            sp.wait_ge(S["o_new_taken"], NH + 1)
            for a in range(2):
                sp.dma_start(late[:, a * KD * T // 2:(a + 1) * KD * T // 2],
                             h_spill[:, a * KD * T // 2:(a + 1) * KD * T // 2]).then_inc(S["h_loaded"], 16)
            sp.wait_ge(S["onew_low"], 1)
            sp.wait_ge(S["pooled_low"], PT)
            sp.dma_start(p_nat, p_prompt[0, 0].rearrange("(b p) n -> p b n", p=P)).then_inc(S["p_landed"], 16)
            sp.dma_start(ps_nat, p_sample[0].rearrange("b s n -> (b s) n")).then_inc(S["p_landed"], 16)
            with sp.Fori(1, KD // 2) as j:
                load(Slab(OUT_N, j), src_out(2 * j))
                load(Slab(OUT_N + 1, j), src_out(2 * j + 1))

            with sp.Fori(0, NCH) as c:
                with sp.Fori(0, CH) as j:
                    for s in (0, 1):
                        load(Slab(FFN_N + s, c * (FFN_STEP // 2) + j),
                             w_gu_v[:, :, ds(s * DFF + (c * CH + j) * P, P)])
                with sp.Fori(0, CH // 2) as i:
                    for s in (0, 1):
                        load(Slab(FFN_N + 2 * CH + s, c * (FFN_STEP // 2) + i),
                             w_dn_v[:, ds(c * CH, CH), ds((2 * i + s) * 4 * P, 4 * P)])

            def load_wp(j):
                sp.dma_start(wp_raw.rearrange("p (k n) -> p k n", k=2), w_pp_v[:, :, ds(j * 2 * P, 2 * P)])\
                    .then_inc(S["wp_landed"], 16)

            sp.wait_ge(S["p_copied"], 1)
            load_wp(0)
            with sp.Fori(0, KD // 2 - 1) as j:
                for s in (0, 1):
                    load(Slab(PLE_N + s, j), w_pg_v[:, :, ds((2 * j + s) * P, P)])
                sp.wait_ge(S["wp_low"], j + 1)
                load_wp(j + 1)
            for m in (KD - 2, KD - 1):
                load(Slab(PLE_N + m), w_pg_v[:, :, m * P:(m + 1) * P])
            sp.wait_ge(S["misc_stored"], 16)
            sp.wait_ge(S["naturals_stored"], 16 * 4)
            sp.wait_ge(S["nat_stored"], 16 * NH)
            sp.wait_ge(S["v_stored"], 16 * NH)
            sp.wait_ge(S["y_stored"], 16 * 5)

        @block.tensor
        def _(pe):
            def mm(o, l, r, start=True, stop=True):
                return pe.matmul(o, l, r, start=start, stop=stop)

            def product(pair, w_high, w_low, x_high, x_low, first, last):
                for n, (w, x) in enumerate(((w_high, x_high), (w_high, x_low), (w_low, x_high))):
                    for a in (0, 1):
                        ins = mm(pair[:, a, 0:HT], w, x[:, a * HT:(a + 1) * HT],
                                 start=first and n == 0, stop=last and n == 2)
                return ins

            def begin(slab, t, first=False):
                pe.wait_ge(S["w_low_done"], slab.index + 1)
                if not first:
                    pe.wait_ge(S["acc_free"], t - 1)

            def part_of(slab, pair, t, ks, waits=None):
                for k in ks:
                    if waits:
                        waits(k)
                    ins = product(pair, wh[slab.slot][:, k * P:(k + 1) * P],
                                  wl[slab.slot][:, k * P:(k + 1) * P],
                                  xh[:, k, :], xl[:, k, :], k == 0, k == KD - 1)
                    if k == KD - 1:
                        ins.then_inc(S["acc_ready"], 1)

            def whole(slab, pair, t, waits=None, first=False):
                begin(slab, t, first)
                part_of(slab, pair, t, range(KD), waits)

            def stats(phase):
                pe.wait_ge(S["pool_summed"], KD * (phase + 1))
                for a in (0, 1):
                    ins = mm(sc[:, a, 0:HT], ones, sum_sq[:, a * HT:(a + 1) * HT])
                ins.then_inc(S["stats_ready"], 1)

            pe.wait_ge(S["setup_landed"], 32)
            for k in range(KD):
                ins = pe.transpose(mbank[:, k * NB:(k + 1) * NB], xs_nat[:, k * P:(k + 1) * P], ident[0:NB, 0:NB])
            ins.then_inc(S["setup_turned"], 1)
            pe.wait_ge(S["gains_landed"], 16 * 11)
            pe.transpose(obank[:, 0:V_ALL], vec_nat, ident[0:V_ALL, 0:V_ALL]).then_inc(S["setup_turned"], 1)

            for k in range(KD):
                if k % 4 == 0:
                    pe.wait_ge(x_landed[k // 4], 16)
                if k >= 2:
                    pe.wait_ge(S["x_copied"], k - 1)
                for b in range(4):
                    ins = pe.transpose(sc[:, k % 2, b * P:(b + 1) * P],
                                       x_nat[k // 4 % 3][:, b, k % 4 * P:(k % 4 + 1) * P], ident)
                ins.then_inc(S["x_turned"], 1)
            pe.wait_ge(S["state_landed"], 16)
            pe.wait_ge(S["gains_ready"], 1)
            for t in range(PT):
                g = t * len(WINDOWS) // PT
                ins = mm(obank[:, t * NB:(t + 1) * NB], region[0:NB * PS, 2048 + t * P:2048 + (t + 1) * P],
                         C[0:NB * PS, C_SEL + g * NB:C_SEL + (g + 1) * NB])
            ins.then_inc(S["state_summed"], 1)
            pe.wait_ge(S["state_ready"], 1)
            pe.wait_ge(S["lam_ready"], 1)
            mm(obank[:, 0:1], ones[0:1, :], lam_d).then_inc(S["neglam_summed"], 1)

            def x_waits(base):
                return lambda k: pe.wait_ge(S["x_low"], base + k + 1)

            def k_natural(j):
                pe.wait_ge(S["rotated"], 2 * j + 1)
                if is_first(j):
                    pe.wait_ge(S["gains_ready"], 1)
                else:
                    pe.wait_ge(S["mail_free"], j)
                for b in range(4):
                    ins = pe.transpose(mbank[:, b * P:(b + 1) * P], k_now[:, b * P:(b + 1) * P], ident)
                ins.then_inc(S["mail_ready"], 1)

            def qk_iteration(j, waits=None, first=False):
                k_slab, q_slab = Slab(0, j), Slab(1, j)
                whole(k_slab, acc[0], 2 * j, waits, first)
                if first:
                    stats(0)
                begin(q_slab, 2 * j + 1, first)
                part_of(q_slab, acc[1], 2 * j + 1, range(0, KD // 2))
                k_natural(j)
                part_of(q_slab, acc[1], 2 * j + 1, range(KD // 2, KD))

            qk_iteration(0, x_waits(0), first=True)
            with pe.Fori(1, NH) as j:
                qk_iteration(j)

            def scores(g, b):
                if b == 0:
                    pe.wait_ge(S["staged"], g + 1)
                pe.wait_ge(S["exped"], 4 * g + b + 1)
                n = (b + 1) * P
                for c in (0, 1):
                    r = slice(c * HD, (c + 1) * HD)
                    ins = mm(sc[:, c, 0:n], q_now[r, b * P:(b + 1) * P], k_now[r, 0:n])
                ins.then_inc(S["scored"], 1)

            def mail_turn(g, e):
                pe.wait_ge(S["mail_free"], mail(g, e))

            def turn_w(g, b):
                pe.wait_ge(S["combined"], 4 * g + b + 2)
                mail_turn(g, E_TR[b])
                for kb in range(b + 1):
                    ins = pe.transpose(mbank[:, kb * P:(kb + 1) * P], w_row[:, kb * P:(kb + 1) * P], ident)
                ins.then_inc(S["mail_ready"], 1)

            def values(g, b):
                pe.wait_ge(S["mail_free"], mail(g, E_TR[b]) + 1)
                if b == 0:
                    pe.wait_ge(S["o_scaled"], g + 1)
                    pe.wait_ge(S["o_new_taken"], g + 1)
                for kb in range(b + 1):
                    ins = mm(obank[:, b * P:(b + 1) * P], w_turn[b % 2][:, kb * P:(kb + 1) * P],
                             v_nat[:, kb * P:(kb + 1) * P], start=kb == 0, stop=kb == b)
                ins.then_inc(S["o_ready"], 1)

            def turn_sample_scores(g):
                pe.wait_ge(S["dotted"], NPG * (g + 1))
                mail_turn(g, E_SAM)
                for n in range(NPG):
                    ins = pe.transpose(mbank[0:16, n * P:(n + 1) * P], s_past[:, n, :], ident)
                ins.then_inc(S["mail_ready"], 1)

            def sample_weights(g):
                pe.wait_ge(S["diff_ready"], g + 2)
                mail_turn(g, E_W)
                for n in range(NPG):
                    mm(mbank[:, n * NH:(n + 1) * NH], e_row[:, n * P:(n + 1) * P], diff16)
                mm(mbank[:, NPG * NH:(NPG + 1) * NH], ones[0:16, :], diff16n).then_inc(S["mail_ready"], 1)

            def sample_values(g, i):
                if i == 0:
                    for n in range(NPG):
                        pe.wait_ge(v_landed[n], 16 * (g + 1))
                mail_turn(g, (E_PV0, E_PV1)[i])
                for n in range(NPG):
                    ins = mm(mbank[0:NH, :], w_past[:, n * NH:(n + 1) * NH], pages_v[:, n, i * 512:(i + 1) * 512],
                             start=n == 0, stop=n == NPG - 1)
                ins.then_inc(S["mail_ready"], 1)

            def turn_sample_values(g):
                pe.wait_ge(S["mail_free"], mail(g, E_PV1) + 1)
                for h in range(NH):
                    ins = (mm if h == 0 else pe.transpose)(
                        obank[:, h * NH:(h + 1) * NH], w_turn[h // 4][0:NH, h % 4 * P:(h % 4 + 1) * P],
                        ident[0:NH, 0:NH])
                ins.then_inc(S["o_new_ready"], 1)

            def turn_o(g):
                pe.wait_ge(S["o_scaled"], g + 2)
                mail_turn(g, E_OT)
                for b in range(4):
                    ins = pe.transpose(mbank[:, b * P:(b + 1) * P], nat[:, b * P:(b + 1) * P], ident)
                ins.then_inc(S["mail_ready"], 1)

            def v_natural(h):
                pe.wait_ge(S["v_ready"], h + 1)
                pe.wait_ge(S["mail_free"], mail(h - 1, E_VN))
                for b in range(4):
                    ins = pe.transpose(mbank[:, b * P:(b + 1) * P], v_now[:, b * P:(b + 1) * P], ident)
                ins.then_inc(S["mail_ready"], 1)

            def attention(g, fill):
                scores(g, 0)
                fill(0)
                turn_sample_scores(g)
                fill(1)
                scores(g, 1)
                fill(2)
                turn_w(g, 0)
                fill(3)
                fill(4)
                scores(g, 2)
                values(g, 0)
                fill(5)
                turn_w(g, 1)
                fill(6)
                values(g, 1)
                sample_weights(g)
                fill(7)
                scores(g, 3)
                turn_w(g, 2)
                fill(8)
                values(g, 2)
                sample_values(g, 0)
                fill(9)
                fill(10)
                fill(11)
                turn_w(g, 3)
                fill(12)
                values(g, 3)
                sample_values(g, 1)
                fill(13)
                fill(14)
                turn_o(g)
                turn_sample_values(g)
                fill(15)

            def decode_start():
                pe.wait_ge(S["new_taken"], 1)
                for h in range(NH):
                    ins = pe.transpose(sc[0:NB, h // 4, h % 4 * P:(h % 4 + 1) * P], q_new[:, h, :], ident)
                ins.then_inc(S["naturals"], 1)
                pe.wait_ge(S["new_products"], 1)
                pe.wait_ge(S["neglam_ready"], 1)
                for b in range(NB):
                    ins = mm(obank[0:16, b:b + 1], prod_new[:, b * 16:(b + 1) * 16], ones[:, 0:1])
                ins.then_inc(S["snew_ready"], 1)

            def vu_iteration(h):
                v_slab, u_slab = Slab(VU_N, h), Slab(VU_N + 1, h)

                def fill(i):
                    slab, t, pair = (v_slab, VU_N + 2 * h, acc[0]) if i < 8 else (u_slab, VU_N + 1 + 2 * h, acc[1])
                    if i % 8 == 0:
                        begin(slab, t)
                    part_of(slab, pair, t, (i % 8 * 2, i % 8 * 2 + 1))
                if is_first(h):
                    for i in range(FILLS):
                        fill(i)
                        if i == 5:
                            decode_start()
                else:
                    attention(h - 1, fill)
                v_natural(h)

            vu_iteration(0)
            with pe.Fori(1, NH) as h:
                vu_iteration(h)

            def pool_out(t):
                g, m = divmod(t, 2)
                slab = Slab(POOL_N)
                if t == 0:
                    pe.wait_ge(S["w_low_done"], POOL_N + 1)
                pe.wait_ge(S["pooled_low"], 2 * g + 2)
                pe.wait_ge(S["acc_free"], POOL_T + t - 1)
                for k in (0, 1):
                    at = (g * 2 + k) * 2 * P + m * P
                    ins = product(acc[t % 2], wh[slab.slot][:, at:at + P], wl[slab.slot][:, at:at + P],
                                  xh[:, 2 * g + k, :], xl[:, 2 * g + k, :], k == 0, k == 1)
                ins.then_inc(S["acc_ready"], 1)

            def out_part(m, ks):
                slab = Slab(OUT_N + m)
                for k in ks:
                    ins = product(acc[m], wh[slab.slot][:, k * P:(k + 1) * P], wl[slab.slot][:, k * P:(k + 1) * P],
                                  xh[:, k, :], xl[:, k, :], k == NH, k == NH - 1)
                    if k == NH - 1:
                        ins.then_inc(S["acc_ready"], 1)

            def last_fill(i):
                if i < PT:
                    pool_out(i)
                else:
                    m, n = divmod(i - PT, 4)
                    if n == 0:
                        begin(Slab(OUT_N + m), OUT_T + m)
                        pe.wait_ge(S["acc_free"], POOL_T + PT)
                    out_part(m, (NH + 2 * n, NH + 2 * n + 1))
            attention(NH - 1, last_fill)

            def natural(i, new, n):
                if i == 0:
                    pe.wait_ge(S["exped"], 4 * NH + 1)
                pe.wait_ge(S["naturals_copied"], i + 1)
                for h in range(NH):
                    ins = pe.transpose(sc[0:n, h // 4, h % 4 * P:(h % 4 + 1) * P], new[:, h, :], ident)
                ins.then_inc(S["naturals"], 1)
            natural(0, k_new, NB)
            pe.wait_ge(S["onew_squared"], 1)
            mm(obank[:, 0:64], ones, v_squares[:, 0:64]).then_inc(S["onew_stats"], 1)
            natural(1, v_new, NB)
            pe.wait_ge(S["o_low_done"], NH)
            pe.wait_ge(S["onew_low"], 1)
            out_part(0, range(NH))
            natural(2, u_new, 23)
            out_part(1, range(NH))

            def out_pair(j):
                whole(Slab(OUT_N, j), acc[0], OUT_T + 2 * j)
                whole(Slab(OUT_N + 1, j), acc[1], OUT_T + 1 + 2 * j)
            out_pair(1)
            pe.wait_ge(S["p_landed"], 32)
            pe.wait_ge(S["naturals_copied"], 4)
            for k in (0, 1):
                bank = (mbank, obank)[k]
                for b in range(4):
                    pe.transpose(bank[:, b * P:(b + 1) * P], p_nat[:, b, k * P:(k + 1) * P], ident)
                ins = pe.transpose(sc[:, 0, k * NB:(k + 1) * NB], ps_nat[:, k * P:(k + 1) * P], ident[0:NB, 0:NB])
            ins.then_inc(S["p_turned"], 1)
            with pe.Fori(2, KD // 2) as j:
                out_pair(j)

            def gate_up(c, j):
                for s in (0, 1):
                    whole(Slab(FFN_N + s, c * (FFN_STEP // 2) + j), acc[s], FFN_T + s + c * FFN_TSTEP + 2 * j)

            def down(c, i):
                for s in (0, 1):
                    slab = Slab(FFN_N + 2 * CH + s, c * (FFN_STEP // 2) + i)
                    order = [(m, k) for m in range(4) for k in range(CH)]
                    if i == 0 and s == 0:
                        order[0:2 * CH] = ([(0, k) for k in range(CH - 1)] + [(1, k) for k in range(CH - 2)]
                                           + [(0, CH - 1), (1, CH - 2), (1, CH - 1)])
                    for m, k in order:
                        t = FFN_T + 2 * CH + 4 * s + m + c * FFN_TSTEP + 8 * i
                        if k == 0 and m == 0:
                            begin(slab, t)
                        elif k == 0:
                            pe.wait_ge(S["acc_free"], t - 1)
                        if i == 0 and s == 0 and m == 0:
                            pe.wait_ge(S["act_low_done"], c * CH + k + 1)
                        at = k * 4 * P + m * P
                        ins = product(acc[m % 2], wh[slab.slot][:, at:at + P], wl[slab.slot][:, at:at + P],
                                      act_h[:, k, :], act_l[:, k, :], k == 0, k == CH - 1)
                        if k == CH - 1:
                            ins.then_inc(S["acc_ready"], 1)

            def first_two(slab0, slab1, t, phase, lead=LEAD):
                waits = x_waits(KD * phase)
                begin(slab0, t)
                part_of(slab0, acc[0], t, range(lead), waits)
                stats(phase)
                begin(slab1, t + 1)
                part_of(slab1, acc[1], t + 1, range(lead))
                for k in range(lead, KD):
                    part_of(slab0, acc[0], t, (k,), waits)
                    if k < KD // 2 + 1:
                        part_of(slab1, acc[1], t + 1, (k,))
                part_of(slab1, acc[1], t + 1, range(KD // 2 + 1, KD))
            pe.wait_ge(S["p_copied"], 1)
            first_two(Slab(FFN_N), Slab(FFN_N + 1), FFN_T, 1)
            with pe.Fori(1, CH) as j:
                gate_up(0, j)
            for i in range(CH // 2):
                down(0, i)
            with pe.Fori(1, NCH) as c:
                with pe.Fori(0, CH) as j:
                    gate_up(c, j)
                for i in range(CH // 2):
                    down(c, i)

            def project(j, s):
                m = 2 * j + s
                if s == 0:
                    pe.wait_ge(S["wp_low"], j + 1)
                if s > 0 or not is_first(j):
                    pe.wait_ge(S["proj_free"], m)
                for k in (0, 1):
                    at = k * 2 * P + s * P
                    ins = product(sc, act_h[:, 2, at:at + P], act_l[:, 2, at:at + P],
                                  act_h[:, k, :], act_l[:, k, :], k == 0, k == 1)
                ins.then_inc(S["proj_ready"], 1)

            def turn_y(m, s):
                pe.wait_ge(S["hg_ready"], m + 1)
                if not is_first(m):
                    pe.wait_ge(S["y_taken"], m)
                for b in range(4):
                    pe.transpose(mbank[:, b * P:(b + 1) * P], hg_row[s][:, b * P:(b + 1) * P], ident)
                pe.transpose(obank[0:NB, 0:P], hg_row[s][:, SEQ:T], ident).then_inc(S["y_turned"], 1)

            def ple(j):
                for s in (0, 1):
                    slab, t = Slab(PLE_N + s, j), PLE_T + s + 2 * j
                    begin(slab, t)
                    part_of(slab, acc[s], t, range(0, KD // 2))
                    turn_y(2 * j + s - 1, 1 - s)
                    part_of(slab, acc[s], t, range(KD // 2, KD))
                    project(j, s)

            first_two(Slab(PLE_N), Slab(PLE_N + 1), PLE_T, 2)
            pe.wait_ge(S["p_low"], 2)
            pe.wait_ge(S["root_ready"], 3)
            project(0, 0)
            project(0, 1)
            turn_y(0, 0)
            with pe.Fori(1, KD // 2) as j:
                ple(j)
            turn_y(KD - 1, 1)
            pe.wait_ge(S["pool_summed"], KD * 4)
            pe.wait_ge(S["proj_free"], KD)
            for b in range(4):
                mm(sc[:, 0, b:b + 1], sum_sq[:, b * P:(b + 1) * P], ones[:, 0:1])
            mm(sc[0:NB, 0, 4:5], sum_sq[:, SEQ:T], ones[:, 0:1]).then_inc(S["fin_stats"], 1)

        @block.scalar
        def _(act):
            A = Steps(act, S["act_step"])

            def high(slab):
                act.wait_ge(raw_landed[slab.slot], 16 * (slab.turn + 1))
                act.activation(wh[slab.slot][:, :], raw[slab.slot][:, :], ACT.Copy).then_inc(S["w_high_done"], 1)

            def square(phase, m, slot):
                if phase or not isinstance(m, int) or m >= 2:
                    act.wait_ge(S["pool_summed"], KD * phase - 1 + m)
                act.activation(sq[slot], h_all[:, ds(m, 1), :].rearrange("p a t -> p (a t)"), ACT.Square).then_inc(S["squared"], 1)

            def x_high(k, gain):
                act.activation(xh[:, k, :], h_all[:, k, :], ACT.Copy,
                               scale=gains[:, gain + k:gain + k + 1]).then_inc(S["x_high"], 1)

            def root(phase):
                act.wait_ge(S["stats_ready"], phase + 1)
                act.activation(halves(rstd[:, :]), sc_t, ACT.Sqrt, scale=1.0 / D, bias=eps).then_inc(S["root_ready"], 1)

            act.wait_ge(S["lam_summed"], 1)
            act.activation(lam_e, lam_s, ACT.Exp).then_inc(S["lam_exped"], 1)
            act.wait_ge(S["gains_ready"], 1)

            for k in range(KD):
                if k == 8:
                    high(Slab(0))
                act.wait_ge(S["x_copied"], k + 1)
                x_high(k, V_MIX)
                square(0, k, k % 2)
            act.wait_ge(S["x_copied"], KD)
            act.dma_start(h_spill, late).then_inc(S["h_spilled"], 16)
            high(Slab(1))
            root(0)

            def swap(t, pair):
                act.wait_ge(S["acc_ready"], t + 1)
                if not is_first(t):
                    act.wait_ge(S["rotated"], t)
                for n in range(4):
                    o = n + 1 - 2 * (n % 2)
                    ins = act.activation(halves(v_now[32 * n:32 * n + 32, :]), pair[32 * o:32 * o + 32, :, 0:HT], ACT.Copy)
                ins.then_inc(S["swapped"], 1)

            def qk_iteration(j, first=False):
                swap(2 * j, acc[0])
                high(Slab(2, j))
                act.wait_ge(S["mail_ready"], j + 1)
                if not first:
                    act.wait_ge(S["nat_stored"], 16 * j)
                A.says(act.activation(v_nat[:, :], mbank[:, :], ACT.Copy), S["mail_free"], j + 1)
                A.wait()
                act.dma_start(k_prompt[0, 0].rearrange("(b p) c d -> p b (c d)", p=P)[:, :, ds(j * P, P)],
                              v_nat[:, :].rearrange("p (b n) -> p b n", b=4)).then_inc(S["nat_stored"], 16)
                swap(2 * j + 1, acc[1])
                high(Slab(3, j))
            qk_iteration(0, first=True)
            with act.Fori(1, NH) as j:
                qk_iteration(j)

            act.wait_ge(S["naturals"], 1)
            act.wait_ge(S["h_spilled"], 16)
            act.activation(qb[0:NB, 0:512], sc[0:NB, 0, :], ACT.Copy).then_inc(S["naturals_copied"], 1)
            act.activation(qb[0:NB, 512:1024], sc[0:NB, 1, :], ACT.Copy).then_inc(S["o_new_taken"], 1)
            act.wait_ge(S["naturals_copied"], 1)
            act.wait_ge(S["o_new_taken"], 1)
            act.dma_start(q_rows, qb[0:NB, :]).then_inc(S["q_stored"], 16)
            act.wait_ge(S["snew_ready"], 1)
            act.activation(s_new, obank[0:16, 0:NB], ACT.Copy).then_inc(S["exped"], 1)

            def take(g, e, dest, src, scale=1.0):
                act.wait_ge(S["mail_ready"], mail(g, e) + 1)
                A.says(act.activation(dest, src, ACT.Copy, scale=scale), S["mail_free"], mail(g, e) + 1)

            def exps(g, b):
                act.wait_ge(S["maxed"], 4 * g + b + 1)
                act.wait_ge(S["combined"], 4 * g + b + 1)
                n = (b + 1) * P
                for c in (0, 1):
                    ins = act.activation(probs[:, c, 0:n], sc[:, c, 0:n], ACT.Exp, bias=top[:, c:c + 1],
                                         scale=SCALE, accum_out=esum[:, c:c + 1])
                ins.then_inc(S["exped"], 1)

            def attention(g, fill):
                fill(0)
                exps(g, 0)
                act.wait_ge(S["diff_ready"], g + 1)
                act.wait_ge(S["mail_ready"], mail(g, E_SAM) + 1)
                A.says(act.activation(s_row[:, 0:PAST], mbank[0:16, :], ACT.Copy), S["mail_free"], mail(g, E_SAM) + 1)
                act.activation(s_row[:, PAST:PAST + 1], s_new[:, ds(g, 1)], ACT.Copy).then_inc(S["s_ready"], 1)
                fill(1)
                exps(g, 1)
                fill(2)
                take(g, E_TR0, w_turn[0][:, 0:P], mbank[:, 0:P])
                fill(3)
                act.wait_ge(S["s_maxed"], g + 1)
                act.activation(e_row, s_row, ACT.Exp, bias=top16, scale=SCALE, accum_out=sum16).then_inc(S["s_exped"], 1)
                fill(4)
                take(g, E_TR1, w_turn[1][:, 0:2 * P], mbank[:, 0:2 * P])
                exps(g, 2)
                fill(5)
                act.wait_ge(S["mail_ready"], mail(g, E_W) + 1)
                A.step(act.activation(w_past[:, 0:NPG * NH], mbank[:, 0:NPG * NH], ACT.Copy))
                A.says(act.activation(w_new[:, ds(g, 1), :], mbank[:, NPG * NH:(NPG + 1) * NH].rearrange("p (a h) -> p a h", a=1),
                                      ACT.Copy), S["mail_free"], mail(g, E_W) + 1)
                fill(6)
                act.wait_ge(S["o_ready"], 4 * g + 1)
                take(g, E_TR2, w_turn[0][:, 0:3 * P], mbank[:, 0:3 * P])
                exps(g, 3)
                fill(7)
                act.wait_ge(S["o_ready"], 4 * g + 3)
                take(g, E_PV0, w_turn[0][0:NH, :], mbank[0:NH, :])
                fill(8)
                take(g, E_TR3, w_turn[1][:, :], mbank[:, :])
                fill(9)
                act.wait_ge(S["o_ready"], 4 * g + 4)
                for b in range(4):
                    ins = act.activation(probs[:, 0, b * P:(b + 1) * P],
                                         obank[:, b * P:(b + 1) * P], ACT.Square, accum_out=o_ss[:, b:b + 1])
                A.step(ins)
                A.wait()
                act.activation(o_root, o_ss, ACT.Sqrt, scale=1.0 / P, bias=eps).then_inc(S["o_squared"], 1)
                take(g, E_PV1, w_turn[1][0:NH, :], mbank[0:NH, :])
                take(g, E_OT, q_all[:, ds(g, 1), 0:SEQ], mbank[:, :].rearrange("p (a n) -> p a n", a=1), scale=gsub)
                act.wait_ge(S["o_new_ready"], g + 1)
                own = obank[:, 0:(NH - 1) * (NH + 1) + 1:NH + 1]
                act.activation(o_new[:, ds(g, 1), :], own.rearrange("p (a h) -> p a h", a=1),
                               ACT.Copy).then_inc(S["o_new_taken"], 1)

            def v_natural(h, first=False):
                act.wait_ge(S["mail_ready"], mail(h - 1, E_VN) + 1)
                if not first:
                    act.wait_ge(S["v_stored"], 16 * h)
                act.activation(v_nat[:, :], mbank[:, :], ACT.Copy).then_inc(S["mail_free"], 1)

            def store_v(h):
                act.wait_ge(S["mail_free"], mail(h - 1, E_VN) + 1)
                act.dma_start(v_prompt[0, 0].rearrange("(b p) c d -> p b (c d)", p=P)[:, :, ds(h * P, P)],
                              v_nat[:, :].rearrange("p (b n) -> p b n", b=4)).then_inc(S["v_stored"], 16)

            def high_u(h):
                act.wait_ge(S["acc_ready"], VU_N + 2 * h)
                high(Slab(VU_N + 1, h))

            def high_v(h):
                act.wait_ge(S["acc_ready"], VU_N + 2 * h + 1)
                high(Slab(VU_N + 2, h))

            act.wait_ge(S["nat_stored"], 16 * NH)
            high_v(0)
            v_natural(0, first=True)
            for h in A.loop(1, NH, 2):
                attention(h - 1, lambda i: high_u(h) if i == 0 else store_v(h - 1) if i == 2 else high_v(h) if i == 7 else None)
                v_natural(h)

            def pooled_high(*ks):
                for k in ks:
                    if k == 0:
                        act.wait_ge(S["acc_ready"], POOL_T)
                    act.wait_ge(S["u_taken"], 2 * k + 2)
                    act.activation(xh[:, k, :], k_all[:, k, :], ACT.Copy).then_inc(S["pooled_high"], 1)

            def pool_out_high(*ts):
                for t in ts:
                    act.wait_ge(S["acc_ready"], POOL_T + t + 1)
                    act.activation(halves(xh[:, NH + t, :]), out(t), ACT.Copy,
                                   scale=gains[:, V_POOL + t:V_POOL + t + 1]).then_inc(S["pool_high"], 1)

            def o_high(*ks):
                act.wait_ge(S["acc_ready"], POOL_T + PT)
                for k in ks:
                    act.activation(xh[:, k, 0:SEQ], q_all[:, k, 0:SEQ], ACT.Copy).then_inc(S["o_high_done"], 1)

            def last_fill(i):
                if i == 0:
                    pooled_high(0, 1)
                elif i == 1:
                    pooled_high(2, 3)
                    pool_out_high(0)
                elif i == 2:
                    store_v(NH - 1)
                    pool_out_high(1)
                    pooled_high(4, 5)
                elif i == 3:
                    pool_out_high(2)
                elif i == 4:
                    pool_out_high(3)
                    pooled_high(6, 7)
                    high_u(NH)
                elif i == 5:
                    pool_out_high(4, 5)
                elif i == 6:
                    pool_out_high(6, 7)
                elif i == 8:
                    act.wait_ge(S["acc_ready"], POOL_T + PT)
                    high(Slab(POOL_N + 2))
                elif i == 9:
                    o_high(*range(NH - 1))
            attention(NH - 1, last_fill)

            def natural(i, dest, n):
                act.wait_ge(S["naturals"], i + 2)
                act.activation(dest[0:n, :].rearrange("p (a n) -> p a n", a=2), sc[0:n, :, :], ACT.Copy).then_inc(S["naturals_copied"], 1)
            act.wait_ge(S["mail_free"], mail(NH - 1, E_OT) + 1)
            o_high(NH - 1)
            natural(0, nat_k, NB)
            act.wait_ge(S["onew_stats"], 1)
            act.activation(v_squares[:, 64:128], obank[:, 0:64], ACT.Sqrt, scale=1.0 / P, bias=eps).then_inc(S["onew_root"], 1)
            natural(1, nat_v, NB)
            act.wait_ge(S["onew_done"], 1)
            act.activation(xh[:, 0:NH, SEQ:T], q_all[:, :, SEQ:T], ACT.Copy).then_inc(S["onew_done"], 1)
            natural(2, nat_u, 23)
            act.wait_ge(S["naturals_copied"], 4)
            act.dma_start(k_sample[0].rearrange("b s c d -> (b s) (c d)"), nat_k[0:NB, :]).then_inc(S["naturals_stored"], 16)
            act.dma_start(v_sample[0].rearrange("b s c d -> (b s) (c d)"), nat_v[0:NB, :]).then_inc(S["naturals_stored"], 16)
            act.dma_start(pool_prompt[0, 0], nat_u[0:PS, :]).then_inc(S["naturals_stored"], 16)
            act.dma_start(pool_sample[0, :, PS - 1, :], nat_u[PS:PS + NB, :]).then_inc(S["naturals_stored"], 16)
            act.wait_ge(S["v_stored"], 16 * NH)

            def after(t, slab):
                act.wait_ge(S["acc_ready"], t + 1)
                high(slab)

            def out_step(j, i, more=True):
                if more:
                    after(OUT_T + i + 2 * j, Slab(OUT_N + i + 2, j))
                act.wait_ge(S["acc_free"], OUT_T + i + 2 * j + 1)
                square(1, 2 * j + i, i)

            def norm_high(phase, gain, slab):
                for k in range(KD):
                    if k == LEAD:
                        high(slab)
                    if k == LEAD + 3:
                        root(phase)
                    x_high(k, gain)
            with act.Fori(0, KD // 2 - 1) as j:
                out_step(j, 0)
                out_step(j, 1)
            out_step(KD // 2 - 1, 0)
            out_step(KD // 2 - 1, 1, more=False)

            norm_high(1, V_FFN, Slab(FFN_N + 1))

            def gate_up(c, j):
                n = FFN_N, c * (FFN_STEP // 2) + j
                number = c * CH + j
                act.wait_ge(S["acc_free"], FFN_T + c * FFN_TSTEP + 2 * j + 1)
                act.activation(silu_row[0], gate_row[0], ACT.Silu).then_inc(S["silued"], 1)
                high(Slab(n[0] + 2, n[1]))
                act.wait_ge(S["act_product"], number + 1)
                act.activation(act_h[:, ds(j, 1), :], act_row.rearrange("p (a t) -> p a t", a=1), ACT.Copy).then_inc(S["act_high_done"], 1)
                high(Slab(n[0] + 3, n[1]))

            def down(c, i, last=False):
                for s in (0, 1):
                    t = FFN_T + 2 * CH + 4 * s + c * FFN_TSTEP + 8 * i
                    if not (last and i == 1 and s == 1):
                        after(t + 3, Slab(FFN_N + 2 * CH + s + 2, c * (FFN_STEP // 2) + i))
                    if last:
                        act.wait_ge(S["acc_free"], t + 4)
                        for m in range(4):
                            square(2, 8 * i + 4 * s + m, m % 2)

            def chunk(c, last=False):
                with act.Fori(0, CH) as j:
                    gate_up(c, j)
                for i in range(CH // 2):
                    down(c, i, last)
            with act.Fori(0, NCH - 1) as c:
                chunk(c)
            chunk(NCH - 1, last=True)

            def wp(j):
                act.wait_ge(S["wp_landed"], 16 * (j + 1))
                if not is_first(j):
                    act.wait_ge(S["proj_ready"], 2 * j)
                act.activation(act_h[:, 2, 0:512], wp_raw, ACT.Copy).then_inc(S["wp_high"], 1)

            for k in (0, 1):
                act.activation(act_h[:, k, :], p_turn[:, k, :], ACT.Copy).then_inc(S["p_high"], 1)
            norm_high(2, V_PLE, Slab(PLE_N + 1))
            wp(0)

            def ple(j, more=True):
                for s in (0, 1):
                    m = 2 * j + s
                    act.wait_ge(S["acc_free"], PLE_T + m + 1)
                    act.activation(silu_row[s], gate_row[s], ACT.Sigmoid).then_inc(S["silued"], 1)
                    if more:
                        high(Slab(PLE_N + s + 2, j))
                    act.wait_ge(S["pool_summed"], KD * 3 + m - 1)
                    act.wait_ge(S["h_done"], m + 1)
                    act.activation(hg_row[s], h_all[:, ds(m, 1), :].rearrange("p a t -> p (a t)"), ACT.Copy,
                                   scale=gains[:, ds(m + V_FINAL, 1)]).then_inc(S["hg_ready"], 1)
                    A.says(act.activation(sq[s], h_all[:, ds(m, 1), :].rearrange("p a t -> p (a t)"), ACT.Square),
                           S["squared"], KD * 3 + m + 1)
                    if s == 1 and more:
                        wp(j + 1)
                    A.wait()
                    act.wait_ge(S["y_turned"], m + 1)
                    act.activation(ys_nat[:, ds(m * P, P)], obank[0:NB, 0:P], ACT.Copy)
                    act.activation(h_all[:, ds(m, 1), 0:SEQ], mbank[:, :].rearrange("p (a n) -> p a n", a=1),
                                   ACT.Copy).then_inc(S["y_taken"], 1)
            with act.Fori(0, KD // 2 - 1) as j:
                ple(j)
            ple(KD // 2 - 1, more=False)

            act.wait_ge(S["fin_stats"], 1)
            act.activation(fin[:, 0:4], sc[:, 0, 0:4], ACT.Sqrt, scale=1.0 / D, bias=eps).then_inc(S["fin_root"], 1)
            act.activation(fin[0:NB, 4:5], sc[0:NB, 0, 4:5], ACT.Sqrt, scale=1.0 / D, bias=eps[0:NB, :]).then_inc(S["fin_root"], 1)
            act.wait_ge(S["fin_inv"], 2)
            act.wait_ge(S["y_taken"], KD)

            def store(b):
                act.dma_start(y_prompt[0, b * P:(b + 1) * P, :].rearrange("p (k n) -> p k n", n=P),
                              h_all[:, :, b * P:(b + 1) * P]).then_inc(S["y_stored"], 16)
            for b in (0, 1):
                blk = h_all[:, :, b * P:(b + 1) * P]
                A.step(act.activation(blk, blk, ACT.Copy, scale=fin[:, 8 + b:9 + b]))
                A.wait()
                store(b)
            for b in (2, 3):
                act.wait_ge(S["y_scaled"], b - 1)
                store(b)
            act.wait_ge(S["y_scaled"], 3)
            act.dma_start(y_sample.rearrange("b s n -> (b s) n"), ys_nat).then_inc(S["y_stored"], 16)

        @block.vector
        def _(dve):
            V = Steps(dve, S["dve_step"])
            tt, stt, ts = dve.tensor_tensor, dve.scalar_tensor_tensor, dve.tensor_scalar

            def low(slab):
                dve.wait_ge(S["w_high_done"], slab.index + 1)
                tt(wl[slab.slot][:, :], raw[slab.slot][:, :], wh[slab.slot][:, :].bitcast(F32),
                   ALU.subtract).then_inc(S["w_low_done"], 1)

            def x_low(k, src, scalar, base):
                dve.wait_ge(S["x_high"], base + k + 1)
                if scalar is None:
                    ins = tt(xl[:, k, :], src, xh[:, k, :].bitcast(F32), ALU.subtract)
                else:
                    ins = stt(out=xl[:, k, :], in0=src, scalar=scalar, in1=xh[:, k, :].bitcast(F32),
                              op0=ALU.mult, op1=ALU.subtract)
                ins.then_inc(S["x_low"], 1)

            def norm_split(phase, gain, base, k):
                x_low(k, h_all[:, k, :], gains[:, gain + k:gain + k + 1], base)

            def invert_root(phase):
                dve.wait_ge(S["root_ready"], phase + 1)
                V.step(dve.reciprocal(rstd[:, :], rstd[:, :]))

            dve.wait_ge(S["gains_landed"], 16 * 11)
            V.step(tt(lam_pr, lam_in[:, 0:4:2, :], lam_in[:, 1:4:2, :], ALU.mult))
            V.wait()
            dve.tensor_reduce(lam_s, lam_pr, AX.X, ALU.add).then_inc(S["lam_summed"], 1)
            dve.wait_ge(S["setup_turned"], 1)
            V.step(dve.tensor_copy(h_all[:, :, SEQ:T], mbank[:, 0:KD * NB].rearrange("p (k b) -> p k b", k=KD)))
            dve.wait_ge(S["setup_turned"], 2)
            V.says(dve.tensor_copy(gains[:, :], obank[:, 0:V_ALL]), S["gains_ready"], 1)
            V.wait()
            V.step(ts(gsub, gains[:, V_SUB:V_SUB + 1], 1.0 - LAM0, None, ALU.mult))
            dve.wait_ge(S["lam_exped"], 1)
            V.step(tt(lam_d, lam_e[:, 1:2], lam_e[:, 0:1], ALU.subtract))
            V.wait()
            ts(lam_d, lam_d, -LAM0, None, ALU.add).then_inc(S["lam_ready"], 1)
            for k in range(KD):
                dve.wait_ge(S["x_turned"], k + 1)
                dve.tensor_copy(h_all[:, k, 0:SEQ], sc[:, k % 2, :]).then_inc(S["x_copied"], 1)
                if k == 9:
                    low(Slab(0))
                if k >= 1:
                    norm_split(0, V_MIX, 0, k - 1)
            norm_split(0, V_MIX, 0, KD - 1)
            dve.wait_ge(S["state_summed"], 1)
            dve.tensor_copy(state_sum, obank[:, 0:PT * NB]).then_inc(S["state_ready"], 1)
            low(Slab(1))
            dve.wait_ge(S["neglam_summed"], 1)
            V.says(dve.tensor_copy(neglam[:, :], obank[:, 0:1]), S["neglam_ready"], 1)
            V.wait()
            V.step(ts(sgnlam, C[0:16, C_SGN + 1:C_SGN + 2], neglam[0:16, :], C[0:16, C_SGN:C_SGN + 1], ALU.mult, ALU.add))
            invert_root(0)
            V.wait()
            dve.wait_ge(S["rope_landed"], 32)
            V.step(tt(cos_r, q_now[:, :], rstd[:, :], ALU.mult))
            V.step(tt(sin_r, nat[:, :], rstd[:, :], ALU.mult))
            V.wait()

            def rotate(t, pair, dest):
                dve.wait_ge(S["swapped"], t + 1)
                V.says(tt(halves(cos_part), pair[:, :, 0:HT], halves(cos_r), ALU.mult), S["acc_free"], t + 1)
                V.step(tt(v_now[:, :], v_now[:, :], sin_r, ALU.mult))
                V.wait()
                tt(dest, cos_part, v_now[:, :], ALU.add).then_inc(S["rotated"], 1)
            cos_part = q_now[:, :]

            def qk_iteration(j, first=False):
                if not first:
                    dve.wait_ge(S["k_stored"], j)
                    dve.wait_ge(S["mail_ready"], j)
                rotate(2 * j, acc[0], k_now[:, :])
                low(Slab(2, j))
                rotate(2 * j + 1, acc[1], q_all[:, ds(j, 1), :].rearrange("p a t -> p (a t)"))
                low(Slab(3, j))
            V.wait()
            saved = V.k
            qk_iteration(0, first=True)
            per = V.k - saved
            for j in V.loop(1, NH, per):
                qk_iteration(j)

            dve.wait_ge(S["rotated"], 2 * NH)
            dve.wait_ge(S["k_stored"], NH)
            V.step(dve.tensor_copy(k_new, k_all[:, :, SEQ:T]))
            V.says(dve.tensor_copy(q_new, q_all[:, :, SEQ:T]), S["new_taken"], 1)
            V.step(dve.memset(prod_new, 0.0))
            V.wait()
            pn = prod_new.rearrange("p (b h c) -> p h b c", b=NB, c=2)
            V.step(tt(pn[0:HD, :, :, 0], q_all[0:HD, :, SEQ:T], k_all[0:HD, :, SEQ:T], ALU.mult))
            tt(pn[HD:P, :, :, 1], q_all[HD:P, :, SEQ:T], k_all[HD:P, :, SEQ:T], ALU.mult).then_inc(S["new_products"], 1)
            dve.memset(u_row[1][:, 0:16], 0.0).then_inc(S["combined"], 1)
            dve.memset(u_row[2][:, 0:16], 0.0).then_inc(S["o_scaled"], 1)
            V.says(dve.memset(u_row[0][:, 0:16], 0.0), S["diff_ready"], 1)
            V.wait()

            def soften(g, b):
                dve.wait_ge(S["scored"], 4 * g + b + 1)
                n = b * P
                mask = C[:, C_MASK:C_MASK + P].rearrange("p (a n) -> p a n", a=1).to_broadcast([P, 2, P])
                V.step(tt(sc[:, :, n:n + P], sc[:, :, n:n + P], mask, ALU.add))
                V.wait()
                V.step(dve.tensor_reduce(einv, sc[:, :, 0:n + P], AX.X, ALU.max))
                V.wait()
                ts(top, einv, -SCALE, None, ALU.mult).then_inc(S["maxed"], 1)

            def combine(g, b, e):
                n = (b + 1) * P
                dve.wait_ge(S["exped"], 4 * g + b + 2)
                V.step(dve.reciprocal(einv, esum))
                V.wait()
                V.step(ts(probs[:, 1, 0:n], probs[:, 1, 0:n], einv[:, 1:2], neglam[:, :], ALU.mult, ALU.mult))
                V.wait()
                dve.wait_ge(S["mail_ready"], mail(g, e) + 1)
                stt(out=w_row[:, 0:n], in0=probs[:, 0, 0:n], scalar=einv[:, 0:1], in1=probs[:, 1, 0:n],
                    op0=ALU.mult, op1=ALU.add).then_inc(S["combined"], 1)

            def dots(g):
                for n in range(NPG):
                    dve.wait_ge(S["multiplied"], NPG * g + n + 1)
                    dve.tensor_reduce(s_past[:, n, :], keys[:, n, :].rearrange("p (h d) -> p h d", d=HD), AX.X,
                                      ALU.add).then_inc(S["dotted"], 1)

            def take_v(h, first=False):
                dve.wait_ge(S["acc_ready"], VU_N + 2 * h + 1)
                if not first:
                    dve.wait_ge(S["mail_ready"], mail(h - 2, E_VN) + 1)
                V.says(tt(halves(v_now[:, :]), acc[0][:, :, 0:HT], halves(rstd[:, :]), ALU.mult), S["acc_free"], VU_N + 2 * h + 1)
                V.wait()
                dve.tensor_copy(v_new[:, ds(h, 1), :], v_now[:, SEQ:T].rearrange("p (a b) -> p a b", a=1)).then_inc(S["v_ready"], 1)

            def take_u(h):
                u = u_row[0]
                dve.wait_ge(S["acc_ready"], VU_N + 2 * h + 2)
                V.says(tt(halves(u[:, 16:16 + T]), acc[1][:, :, 0:HT], halves(rstd[:, :]), ALU.mult), S["acc_free"], VU_N + 2 * h + 2)

            def pool_u(h):
                u, a, b = u_row
                dve.wait_ge(S["acc_free"], VU_N + 2 * h + 2)
                col = [C[:, ds(4 * h + C_WIN + i, 1)] for i in range(4)]
                dve.tensor_copy(u_new[:, ds(h, 1), :], u[:, 16 + SEQ - PS:16 + T].rearrange("p (a b) -> p a b", a=1)).then_inc(S["u_taken"], 1)
                V.step(tt(a[:, 16:528], u[:, 16:528], u[:, 15:527], ALU.add))
                V.wait()
                V.step(stt(out=b[:, 16:528], in0=a[:, 14:526], scalar=col[0], in1=a[:, 16:528], op0=ALU.mult, op1=ALU.add))
                V.wait()
                V.step(stt(out=a[:, 16:528], in0=b[:, 12:524], scalar=col[1], in1=b[:, 16:528], op0=ALU.mult, op1=ALU.add))
                V.wait()
                V.step(stt(out=b[:, 16:528], in0=a[:, 8:520], scalar=col[2], in1=a[:, 16:528], op0=ALU.mult, op1=ALU.add))
                V.step(tt(b[:, 528:536], u[:, 528:536], state_sum[:, ds(h * NB, NB)], ALU.add))
                V.wait()
                V.step(tt(a[:, 16:32], b[:, 16:32], C[:, ds(h * 16 + C_INV, 16)], ALU.mult))
                V.wait()
                dve.wait_ge(S["staged"], h + 1)
                dest = k_all[:, ds(h, 1), :].rearrange("p a t -> p (a t)")
                V.step(tt(dest[:, 0:16], a[:, 16:32], u[:, 16:32], ALU.subtract))
                stt(out=dest[:, 16:T], in0=b[:, 32:536], scalar=col[3], in1=u[:, 32:536], op0=ALU.mult,
                    op1=ALU.subtract).then_inc(S["u_taken"], 1)

            def sample_max(g):
                dve.wait_ge(S["s_ready"], g + 1)
                V.step(dve.tensor_reduce(inv16, s_row, AX.X, ALU.max))
                V.wait()
                ts(top16, inv16, -SCALE, None, ALU.mult).then_inc(S["s_maxed"], 1)

            def sample_diff(g):
                dve.wait_ge(S["s_exped"], g + 1)
                V.step(dve.reciprocal(inv16, sum16))
                V.wait()
                V.step(tt(inv16, inv16, sgnlam, ALU.mult))
                V.wait()
                dve.wait_ge(S["mail_ready"], mail(g - 1, E_W) + 1)
                V.step(ts(diff16, C[0:16, C_PAIR:C_PAIR + NH], inv16, None, ALU.mult))
                V.wait()
                ts(diff16n, diff16, e_row[:, PAST:PAST + 1], None, ALU.mult).then_inc(S["diff_ready"], 1)

            def scale_o(g):
                dve.wait_ge(S["o_squared"], g + 1)
                V.step(dve.reciprocal(o_inv, o_root))
                V.wait()
                dve.wait_ge(S["mail_ready"], mail(g - 1, E_OT) + 1)
                tt(nat[:, 0:SEQ].rearrange("p (b e) -> p b e", b=4), obank[:, :].rearrange("p (b e) -> p b e", b=4),
                   o_inv.rearrange("p (b a) -> p b a", a=1).to_broadcast([P, 4, P]), ALU.mult).then_inc(S["o_scaled"], 1)

            def attention(g, fill):
                soften(g, 0)
                fill(0)
                combine(g, 0, E_TR3 - EV)
                sample_max(g)
                fill(1)
                soften(g, 1)
                fill(2)
                sample_diff(g)
                combine(g, 1, E_TR0)
                fill(3)
                soften(g, 2)
                fill(4)
                combine(g, 2, E_TR1)
                fill(5)
                soften(g, 3)
                fill(6)
                combine(g, 3, E_TR2)
                fill(7)
                scale_o(g)

            def vu_fill(h):
                def fill(i):
                    if i == 0:
                        take_u(h - 1)
                        low(Slab(VU_N + 1, h))
                    elif i == 6:
                        take_v(h)
                    elif i == 7:
                        low(Slab(VU_N + 2, h))
                        pool_u(h - 1)
                        dots(h)
                return fill
            take_v(0, True)
            low(Slab(VU_N + 2))
            dots(0)
            STEPS_VU = 4 * 4 + 1 + 3 + 1 + 7
            for h in V.loop(1, NH, STEPS_VU):
                attention(h - 1, vu_fill(h))

            def pooled_low(*ks):
                for k in ks:
                    dve.wait_ge(S["pooled_high"], k + 1)
                    tt(xl[:, k, :], k_all[:, k, :], xh[:, k, :].bitcast(F32), ALU.subtract).then_inc(S["pooled_low"], 1)

            def pool_out_low(*ts):
                for t in ts:
                    dve.wait_ge(S["pool_high"], t + 1)
                    stt(out=halves(xl[:, NH + t, :]), in0=out(t), scalar=gains[:, V_POOL + t:V_POOL + t + 1],
                        in1=halves(xh[:, NH + t, :].bitcast(F32)), op0=ALU.mult,
                        op1=ALU.subtract).then_inc(S["acc_free"], 1)

            def o_low(*ks):
                for k in ks:
                    dve.wait_ge(S["o_high_done"], k + 1)
                    tt(xl[:, k, 0:SEQ], q_all[:, k, 0:SEQ], xh[:, k, 0:SEQ].bitcast(F32), ALU.subtract).then_inc(S["o_low_done"], 1)

            def last_fill(i):
                if i == 0:
                    take_u(NH - 1)
                    pooled_low(0, 1)
                elif i == 1:
                    pooled_low(2, 3)
                    pool_out_low(0)
                elif i == 2:
                    pool_out_low(1)
                    pooled_low(4, 5)
                    pool_out_low(2)
                    pool_u(NH - 1)
                elif i == 3:
                    pool_out_low(3)
                elif i == 4:
                    pooled_low(6, 7)
                    low(Slab(VU_N + 1, NH))
                elif i == 5:
                    pool_out_low(4, 5, 6, 7)
                elif i == 7:
                    low(Slab(POOL_N + 2))
                    o_low(*range(NH - 1))
            attention(NH - 1, last_fill)

            dve.wait_ge(S["o_new_taken"], NH + 1)
            w_hb = w_new.rearrange("p b h -> p h b")
            o_hb = o_new.rearrange("p b h -> p h b")
            V.step(tt(prod_new[:, 0:64].rearrange("p (h b) -> p h b", h=NH), w_hb, v_new, ALU.mult))
            V.wait()
            V.step(tt(prod_new[:, 64:128].rearrange("p (h b) -> p h b", h=NH), o_hb,
                      prod_new[:, 0:64].rearrange("p (h b) -> p h b", h=NH), ALU.add))
            V.wait()
            tt(v_squares[:, 0:64], prod_new[:, 64:128], prod_new[:, 64:128], ALU.mult).then_inc(S["onew_squared"], 1)
            dve.wait_ge(S["onew_root"], 1)
            V.step(dve.reciprocal(v_squares[:, 0:64], v_squares[:, 64:128]))
            V.wait()
            stt(out=q_all[:, :, SEQ:T], in0=prod_new[:, 64:128].rearrange("p (h b) -> p h b", h=NH), scalar=gsub,
                in1=v_squares[:, 0:64].rearrange("p (h b) -> p h b", h=NH), op0=ALU.mult,
                op1=ALU.mult).then_inc(S["onew_done"], 1)

            o_low(NH - 1)
            dve.wait_ge(S["onew_done"], 2)
            tt(xl[:, 0:NH, SEQ:T], q_all[:, :, SEQ:T], xh[:, 0:NH, SEQ:T].bitcast(F32), ALU.subtract).then_inc(S["onew_low"], 1)

            def add_h(t, pair, m):
                dve.wait_ge(S["acc_ready"], t + 1)
                tile = halves(h_all[:, ds(m, 1), :].rearrange("p a t -> p (a t)"))
                tt(tile, pair[:, :, 0:HT], tile, ALU.add).then_inc(S["acc_free"], 1)

            dve.wait_ge(S["h_loaded"], 32)

            def out_step(j, s, more=True):
                add_h(OUT_T + s + 2 * j, acc[s], 2 * j + s)
                if more:
                    low(Slab(OUT_N + s + 2, j))

            def norm_low(phase, gain, slab):
                for k in range(KD):
                    if k == LEAD:
                        low(slab)
                    if k == LEAD + 3:
                        invert_root(phase)
                    norm_split(phase, gain, KD * phase, k)
                V.wait()
            for j in (0, 1):
                out_step(j, 0)
                out_step(j, 1)
            dve.wait_ge(S["p_turned"], 1)
            V.step(dve.tensor_copy(p_turn[:, 0, 0:SEQ], mbank[:, :]))
            V.step(dve.tensor_copy(p_turn[:, 1, 0:SEQ], obank[:, :]))
            dve.tensor_copy(p_turn[:, :, SEQ:T], sc[:, 0, 0:2 * NB].rearrange("p (k b) -> p k b", k=2)).then_inc(S["p_copied"], 1)
            with dve.Fori(2, KD // 2 - 1) as j:
                out_step(j, 0)
                out_step(j, 1)
            out_step(KD // 2 - 1, 0)
            out_step(KD // 2 - 1, 1, more=False)

            norm_low(1, V_FFN, Slab(FFN_N + 1))

            LAST = CH - 1

            def gate_up(c, j):
                t = FFN_T + c * FFN_TSTEP + 2 * j
                number = c * CH + j
                dve.wait_ge(S["acc_ready"], t + 1)
                V.says(tt(halves(gate_row[0]), acc[0][:, :, 0:HT], halves(rstd[:, :]), ALU.mult), S["acc_free"], t + 1)
                low(Slab(FFN_N + 2, c * (FFN_STEP // 2) + j))
                dve.wait_ge(S["acc_ready"], t + 2)
                V.says(tt(halves(up_row), acc[1][:, :, 0:HT], halves(rstd[:, :]), ALU.mult), S["acc_free"], t + 2)
                V.wait()
                dve.wait_ge(S["silued"], number + 1)
                V.says(tt(act_row, up_row, silu_row[0], ALU.mult), S["act_product"], number + 1)
                V.wait()
                dve.wait_ge(S["act_high_done"], number + 1)
                tt(act_l[:, ds(j, 1), :], act_row.rearrange("p (a t) -> p a t", a=1), act_h[:, ds(j, 1), :].bitcast(F32),
                   ALU.subtract).then_inc(S["act_low_done"], 1)
                if not isinstance(j, int):
                    low(Slab(FFN_N + 3, c * (FFN_STEP // 2) + j))

            def down(c, i, last=False):
                for s in (0, 1):
                    for m in range(4):
                        add_h(FFN_T + 2 * CH + 4 * s + m + c * FFN_TSTEP + 8 * i, acc[m % 2], 8 * i + 4 * s + m)
                        if i == 0 and s == 0 and m == 1:
                            low(Slab(FFN_N + 3, c * (FFN_STEP // 2) + LAST))
                    if not (last and i == 1 and s == 1):
                        low(Slab(FFN_N + 2 * CH + s + 2, c * (FFN_STEP // 2) + i))

            def chunk(c, last=False):
                with dve.Fori(0, LAST) as j:
                    gate_up(c, j)
                gate_up(c, LAST)
                for i in range(CH // 2):
                    down(c, i, last)
            with dve.Fori(0, NCH - 1) as c:
                chunk(c)
            chunk(NCH - 1, last=True)

            def wp_low(j):
                dve.wait_ge(S["wp_high"], j + 1)
                tt(act_l[:, 2, 0:512], wp_raw, act_h[:, 2, 0:512].bitcast(F32), ALU.subtract).then_inc(S["wp_low"], 1)
            for k in (0, 1):
                dve.wait_ge(S["p_high"], k + 1)
                tt(act_l[:, k, :], p_turn[:, k, :], act_h[:, k, :].bitcast(F32), ALU.subtract).then_inc(S["p_low"], 1)
            norm_low(2, V_PLE, Slab(PLE_N + 1))
            wp_low(0)

            def ple(j, more=True):
                for s in (0, 1):
                    m = 2 * j + s
                    t = PLE_T + s + 2 * j
                    dve.wait_ge(S["acc_ready"], t + 1)
                    V.says(tt(halves(gate_row[s]), acc[s][:, :, 0:HT], halves(rstd[:, :]), ALU.mult), S["acc_free"], t + 1)
                    dve.wait_ge(S["proj_ready"], m + 1)
                    dve.wait_ge(S["silued"], NCH * CH + m + 1)
                    V.says(tt(halves(up_row), sc_t, halves(silu_row[s]), ALU.mult), S["proj_free"], m + 1)
                    V.wait()
                    tile = h_all[:, ds(m, 1), :].rearrange("p a t -> p (a t)")
                    tt(tile, tile, up_row, ALU.add).then_inc(S["h_done"], 1)
                    if more:
                        low(Slab(PLE_N + s + 2, j))
                    if s == 1 and more:
                        wp_low(j + 1)
            with dve.Fori(0, KD // 2 - 1) as j:
                ple(j)
            ple(KD // 2 - 1, more=False)
            dve.wait_ge(S["fin_root"], 2)
            dve.reciprocal(fin[:, 8:12], fin[:, 0:4]).then_inc(S["fin_inv"], 1)
            dve.reciprocal(fin[0:NB, 12:13], fin[0:NB, 4:5]).then_inc(S["fin_inv"], 1)
            dve.wait_ge(S["fin_inv"], 2)
            dve.wait_ge(S["y_taken"], KD)
            for b in (2, 3):
                blk = h_all[:, :, b * P:(b + 1) * P]
                ts(blk, blk, fin[:, 8 + b:9 + b], None, ALU.mult).then_inc(S["y_scaled"], 1)
            ts(ys_nat, ys_nat, fin[0:NB, 12:13], None, ALU.mult).then_inc(S["y_scaled"], 1)

        @block.gpsimd
        def _(pool):
            def copy(o, i):
                return pool.tensor_copy(o, i)

            def add_squares(phase):
                pool.memset(sum_sq, 0.0).then_inc(S["pool_step"], 1)
                pool.wait_ge(S["pool_step"], phase + 1)

                def add(m, slot, first=False):
                    pool.wait_ge(S["squared"], KD * phase + m + 1)
                    if not first:
                        pool.wait_ge(S["pool_summed"], KD * phase + m)
                    pool.tensor_tensor(sum_sq, sum_sq, sq[slot], ALU.add).then_inc(S["pool_summed"], 1)
                add(0, 0, first=phase == 0)
                add(1, 1)
                with pool.Fori(1, KD // 2) as j:
                    add(2 * j, 0)
                    add(2 * j + 1, 1)
            add_squares(0)
            with pool.Fori(0, NH) as j:
                pool.wait_ge(S["rotated"], 2 * j + 1)
                copy(k_all[:, ds(j, 1), :].rearrange("p a t -> p (a t)"), k_now[:, :]).then_inc(S["k_stored"], 1)

            def stage(h):
                copy(q_now[:, :], q_all[:, ds(h, 1), :].rearrange("p a t -> p (a t)"))
                copy(k_now[:, :], k_all[:, ds(h, 1), :].rearrange("p a t -> p (a t)")).then_inc(S["staged"], 1)

            def multiply(g):
                pool.wait_ge(S["qb_landed"], 16 * (g + 1))
                for n in range(NPG):
                    pool.wait_ge(k_landed[n], 16 * (g + 1))
                    pool.tensor_tensor(keys[:, n, :], keys[:, n, :], qb, ALU.mult).then_inc(S["multiplied"], 1)
            pool.wait_ge(S["rotated"], 2 * NH)
            pool.wait_ge(S["k_stored"], NH)
            pool.wait_ge(S["mail_ready"], NH)
            stage(0)
            multiply(0)
            with pool.Fori(1, NH) as h:
                multiply(h)
                pool.wait_ge(S["scored"], 4 * h)
                stage(h)
            for phase in (1, 2, 3):
                pool.wait_ge(S["stats_ready"], phase)
                pool.wait_ge(S["u_taken"], 2 * NH)
                add_squares(phase)


_INS = ["x_prompt", "x_sample", "p_prompt", "p_sample", "cache_k", "cache_v", "state_pool", "page_table",
        "g_mix", "w_in", "w_out", "lambda_q1", "lambda_k1", "lambda_q2", "lambda_k2", "g_sub", "w_pool",
        "pool_scale", "g_ffn", "w_gate_up", "w_down", "g_ple", "w_ple_gate", "w_ple_proj", "g_final"]
_OUTS = [(1, SEQ, D), (NB, 1, D), (1, 1, SEQ, 2 * NH, HD), (1, 1, SEQ, NH, P), (1, 1, PS, PW),
         (1, NB, 1, 2 * NH, HD), (1, NB, 1, NH, P), (1, NB, PS, PW)]


def kernel(**inputs):
    import concourse.bacc as bacc
    from concourse.bass_utils import run_bass_kernel_spmd as run

    nc = bacc.Bacc("TRN2", target_bir_lowering=False, num_devices=1, dynamic_dma_scratch_size=512)
    arrays, args = {}, []
    given = [(n, np.ascontiguousarray(inputs[n])) for n in _INS]
    for name, a in given + [("const", constants()), ("rope", rope_tables())]:
        arrays[f"in_{name}"] = a
        args.append(nc.dram_tensor(f"in_{name}", a.shape, mybir.dt.from_np(a.dtype), kind="ExternalInput").ap())
    for i, shape in enumerate(_OUTS):
        args.append(nc.dram_tensor(f"out_{i}", shape, F32, kind="ExternalOutput").ap())
    layer(nc, *args)
    r = run(nc, [arrays], core_ids=[0])
    return tuple(r.results[0][f"out_{i}"] for i in range(len(_OUTS)))
```
